# Optimizing a Trainium2 kernel written in Bass

```python
import math
import jax
import jax.numpy as jnp
from jax import lax
import numpy as np

D_MODEL = 1024
BATCH = 1
SEQ = 2048
DEPTH = 1

N_MIXERS = 2
N_DIFF_LAYERS = (DEPTH + N_MIXERS - 1) // N_MIXERS
N_RET_LAYERS = DEPTH // N_MIXERS

DIFF_HEADS = 8
DIFF_HEAD_DIM = D_MODEL // DIFF_HEADS // 2
DIFF_V_DIM = 2 * DIFF_HEAD_DIM
Q_BLOCK = 128

NUM_BUCKETS = 32
MAX_EXACT = NUM_BUCKETS // 2
MAX_DISTANCE = 128

RET_HEADS = 4
RET_QK_DIM = D_MODEL
RET_HEAD_DK = RET_QK_DIM // RET_HEADS
RET_V_DIM = 2 * D_MODEL
RET_HEAD_DV = RET_V_DIM // RET_HEADS
RET_CHUNK = 128
RET_IN_DIM = 2 * RET_QK_DIM + 2 * RET_V_DIM

N_GROUPS = 4
EXPERTS_PER_GROUP = 8
N_EXPERTS = N_GROUPS * EXPERTS_PER_GROUP
TOP_K_INNER = 2
EXPERT_FF = D_MODEL // 2
ROW_BLOCK = 128

RMS_EPS = 1e-6
SUBLN_EPS = 1e-5

kernel_name = "hybrid_diffattn_retnet_hmoe"

def rms_norm(x, g, eps=RMS_EPS):
    xf = x.astype(jnp.float32)
    y = xf * lax.rsqrt(jnp.mean(xf * xf, axis=-1, keepdims=True) + eps)
    return (y * g.astype(jnp.float32)).astype(x.dtype)

def t5_bucket(rel):
    n = jnp.maximum(rel, 0)
    is_small = n < MAX_EXACT
    nf = jnp.maximum(n, MAX_EXACT).astype(jnp.float32)
    large = MAX_EXACT + (jnp.log(nf / MAX_EXACT) / math.log(MAX_DISTANCE / MAX_EXACT)
                         * (NUM_BUCKETS - MAX_EXACT)).astype(jnp.int32)
    large = jnp.minimum(large, NUM_BUCKETS - 1)
    return jnp.where(is_small, n, large)

def diff_lambda_init(layer_idx):
    return 0.8 - 0.6 * math.exp(-0.3 * layer_idx)

def differential_attention(h, w_in, lam_qk, subln_g, w_out, rel_table, lambda_init):
    B, S, D = h.shape
    proj = h @ w_in
    q, k, v = jnp.split(proj, [D, 2 * D], axis=-1)
    q = q.reshape(B, S, DIFF_HEADS, 2, DIFF_HEAD_DIM).transpose(3, 0, 2, 1, 4)
    k = k.reshape(B, S, DIFF_HEADS, 2, DIFF_HEAD_DIM).transpose(3, 0, 2, 1, 4)
    v = v.reshape(B, S, DIFF_HEADS, DIFF_V_DIM).transpose(0, 2, 1, 3)
    lq = lam_qk.astype(jnp.float32)
    lam = (jnp.exp(jnp.sum(lq[0] * lq[1])) - jnp.exp(jnp.sum(lq[2] * lq[3]))
           + lambda_init)
    scale = DIFF_HEAD_DIM ** -0.5
    nb = S // Q_BLOCK
    qb = q.reshape(2, B, DIFF_HEADS, nb, Q_BLOCK, DIFF_HEAD_DIM).transpose(3, 0, 1, 2, 4, 5)
    kpos = jnp.arange(S)

    def block(args):
        qblk, bi = args
        qpos = bi * Q_BLOCK + jnp.arange(Q_BLOCK)
        rel = qpos[:, None] - kpos[None, :]
        bias = rel_table[t5_bucket(rel)].transpose(2, 0, 1).astype(jnp.float32)
        s = jnp.einsum('ibhqd,ibhkd->ibhqk', qblk, k).astype(jnp.float32) * scale + bias
        s = jnp.where(rel >= 0, s, -jnp.inf)
        p = jax.nn.softmax(s, axis=-1)
        a = p[0] - lam * p[1]
        return jnp.einsum('bhqk,bhkd->bhqd', a.astype(v.dtype), v)

    o = lax.map(block, (qb, jnp.arange(nb)))
    o = o.transpose(1, 0, 3, 2, 4).reshape(B, S, DIFF_HEADS, DIFF_V_DIM)
    o = rms_norm(o, subln_g, SUBLN_EPS) * (1.0 - lambda_init)
    return o.reshape(B, S, D) @ w_out

def rotate_every_two(x):
    x1 = x[..., ::2]
    x2 = x[..., 1::2]
    return jnp.stack((-x2, x1), axis=-1).reshape(x.shape)

def retention_chunkwise(q, k, v):
    B, H, S, DK = q.shape
    DV = v.shape[-1]
    C = RET_CHUNK
    N = S // C
    log_gamma = jnp.log(1.0 - 2.0 ** (-5.0 - jnp.arange(H, dtype=jnp.float32)))
    pos = jnp.arange(C, dtype=jnp.float32)
    dist = pos[:, None] - pos[None, :]
    inner_decay = jnp.where(dist[None] >= 0,
                            jnp.exp(jnp.maximum(dist, 0.0)[None] * log_gamma[:, None, None]),
                            0.0)
    q_decay = jnp.exp((pos + 1.0)[None] * log_gamma[:, None])
    k_decay = jnp.exp((C - 1.0 - pos)[None] * log_gamma[:, None])
    chunk_decay = jnp.exp(C * log_gamma)
    qc = q.reshape(B, H, N, C, DK)
    kc = k.reshape(B, H, N, C, DK)
    vc = v.reshape(B, H, N, C, DV)
    scores = jnp.einsum('bhncd,bhnmd->bhncm', qc, kc) * inner_decay[None, :, None]
    inner = jnp.einsum('bhncm,bhnmv->bhncv', scores, vc)

    def step(state, xs):
        qn, kn, vn = xs
        cross = jnp.einsum('bhcd,bhdv->bhcv', qn * q_decay[None, :, :, None], state)
        state = (state * chunk_decay[None, :, None, None]
                 + jnp.einsum('bhcd,bhcv->bhdv', kn * k_decay[None, :, :, None], vn))
        return state, cross

    xs = (qc.transpose(2, 0, 1, 3, 4), kc.transpose(2, 0, 1, 3, 4), vc.transpose(2, 0, 1, 3, 4))
    _, cross = lax.scan(step, jnp.zeros((B, H, DK, DV), jnp.float32), xs)
    cross = cross.transpose(1, 2, 0, 3, 4)
    return (inner + cross).reshape(B, H, S, DV)

def retention(h, w_in, w_out):
    B, S, D = h.shape
    proj = h @ w_in
    q, k, v, g = jnp.split(proj, [RET_QK_DIM, 2 * RET_QK_DIM, 2 * RET_QK_DIM + RET_V_DIM], axis=-1)
    q = q.reshape(B, S, RET_HEADS, RET_HEAD_DK).transpose(0, 2, 1, 3).astype(jnp.float32)
    k = k.reshape(B, S, RET_HEADS, RET_HEAD_DK).transpose(0, 2, 1, 3).astype(jnp.float32)
    k = k * (RET_HEAD_DK ** -0.5)
    v = v.reshape(B, S, RET_HEADS, RET_HEAD_DV).transpose(0, 2, 1, 3).astype(jnp.float32)
    angle = 1.0 / (10000.0 ** jnp.linspace(0.0, 1.0, RET_HEAD_DK // 2, dtype=jnp.float32))
    angle = jnp.repeat(angle, 2)
    phase = jnp.arange(S, dtype=jnp.float32)[:, None] * angle[None, :]
    sin, cos = jnp.sin(phase), jnp.cos(phase)
    q = q * cos + rotate_every_two(q) * sin
    k = k * cos + rotate_every_two(k) * sin
    o = retention_chunkwise(q, k, v)
    o = o * lax.rsqrt(jnp.mean(o * o, axis=-1, keepdims=True) + RMS_EPS)
    o = o.transpose(0, 2, 1, 3).reshape(B, S, RET_V_DIM).astype(h.dtype)
    o = jax.nn.silu(g) * o
    return o @ w_out

def hierarchical_moe(h, w_group, b_group, w_expert, b_expert, w_gate, w_up, w_down):
    B, S, D = h.shape
    T = B * S
    ht = h.reshape(T, D)
    tok = jnp.arange(T)
    g_probs = jax.nn.softmax((ht @ w_group + b_group).astype(jnp.float32), axis=-1)
    g_idx = jnp.argmax(g_probs, axis=-1)
    g_p = jnp.max(g_probs, axis=-1)
    e_logits = (ht @ w_expert + b_expert).astype(jnp.float32).reshape(T, N_GROUPS, EXPERTS_PER_GROUP)
    e_sel = e_logits[tok, g_idx]
    top_v, top_i = lax.top_k(e_sel, TOP_K_INNER)
    top_w = jax.nn.softmax(top_v, axis=-1) * g_p[:, None]
    expert_id = (g_idx[:, None] * EXPERTS_PER_GROUP + top_i).reshape(-1)
    weight = top_w.reshape(-1)
    token = jnp.repeat(tok, TOP_K_INNER)
    order = jnp.argsort(expert_id)
    s_e, s_tok, s_w = expert_id[order], token[order], weight[order]
    counts = jnp.zeros((N_EXPERTS,), jnp.int32).at[expert_id].add(1)
    padded = ((counts + ROW_BLOCK - 1) // ROW_BLOCK) * ROW_BLOCK
    pad_end = jnp.cumsum(padded)
    pad_start = pad_end - padded
    start = jnp.cumsum(counts) - counts
    n_assign = T * TOP_K_INNER
    dest = pad_start[s_e] + (jnp.arange(n_assign) - start[s_e])
    n_blocks = (n_assign + ROW_BLOCK - 1) // ROW_BLOCK + N_EXPERTS
    n_rows = n_blocks * ROW_BLOCK
    row_tok = jnp.zeros((n_rows,), jnp.int32).at[dest].set(s_tok.astype(jnp.int32))
    row_w = jnp.zeros((n_rows,), jnp.float32).at[dest].set(s_w)
    block_e = jnp.clip(jnp.searchsorted(pad_end, jnp.arange(n_blocks) * ROW_BLOCK, side='right'),
                       0, N_EXPERTS - 1)
    xr = ht[row_tok].reshape(n_blocks, ROW_BLOCK, D)

    def expert_block(args):
        xb, e = args
        return (jax.nn.silu(xb @ w_gate[e]) * (xb @ w_up[e])) @ w_down[e]

    yr = lax.map(expert_block, (xr, block_e)).reshape(n_rows, D)
    y = jnp.zeros((T, D), h.dtype).at[row_tok].add(yr * row_w[:, None].astype(h.dtype))
    return y.reshape(B, S, D)

def setup_inputs(seed: int = 0) -> dict:
    key = jax.random.key(seed)
    ks = jax.random.split(key, 20)

    def nrm(k, shape, scale):
        return jax.random.normal(k, shape, jnp.float32) * scale

    return {
        "x": nrm(ks[0], (BATCH, SEQ, D_MODEL), 1.0),
        "rel_bias_table": nrm(ks[1], (NUM_BUCKETS, DIFF_HEADS), 0.2),
        "norm_mix": 1.0 + nrm(ks[2], (DEPTH, D_MODEL), 0.01),
        "norm_ffn": 1.0 + nrm(ks[3], (DEPTH, D_MODEL), 0.01),
        "norm_final": 1.0 + nrm(ks[4], (D_MODEL,), 0.01),
        "diff_w_in": nrm(ks[5], (N_DIFF_LAYERS, D_MODEL, 3 * D_MODEL), D_MODEL ** -0.5),
        "diff_lambda_qk": nrm(ks[6], (N_DIFF_LAYERS, 4, DIFF_HEAD_DIM), 0.1),
        "diff_subln": 1.0 + nrm(ks[7], (N_DIFF_LAYERS, DIFF_V_DIM), 0.01),
        "diff_w_out": nrm(ks[8], (N_DIFF_LAYERS, D_MODEL, D_MODEL), D_MODEL ** -0.5),
        "ret_w_in": nrm(ks[9], (N_RET_LAYERS, D_MODEL, RET_IN_DIM), D_MODEL ** -0.5),
        "ret_w_out": nrm(ks[10], (N_RET_LAYERS, RET_V_DIM, D_MODEL), RET_V_DIM ** -0.5),
        "moe_w_group": nrm(ks[11], (DEPTH, D_MODEL, N_GROUPS), D_MODEL ** -0.5),
        "moe_b_group": nrm(ks[12], (DEPTH, N_GROUPS), 0.01),
        "moe_w_expert": nrm(ks[13], (DEPTH, D_MODEL, N_EXPERTS), D_MODEL ** -0.5),
        "moe_b_expert": nrm(ks[14], (DEPTH, N_EXPERTS), 0.01),
        "moe_w_gate": nrm(ks[15], (DEPTH, N_EXPERTS, D_MODEL, EXPERT_FF), D_MODEL ** -0.5),
        "moe_w_up": nrm(ks[16], (DEPTH, N_EXPERTS, D_MODEL, EXPERT_FF), D_MODEL ** -0.5),
        "moe_w_down": nrm(ks[17], (DEPTH, N_EXPERTS, EXPERT_FF, D_MODEL), EXPERT_FF ** -0.5),
    }

def reference(x, rel_bias_table, norm_mix, norm_ffn, norm_final, diff_w_in, diff_lambda_qk,
              diff_subln, diff_w_out, ret_w_in, ret_w_out, moe_w_group, moe_b_group,
              moe_w_expert, moe_b_expert, moe_w_gate, moe_w_up, moe_w_down):
    for i in range(DEPTH):
        hn = rms_norm(x, norm_mix[i])
        j = i // N_MIXERS
        if i % N_MIXERS == 0:
            mix = differential_attention(hn, diff_w_in[j], diff_lambda_qk[j], diff_subln[j],
                                         diff_w_out[j], rel_bias_table, diff_lambda_init(i))
        else:
            mix = retention(hn, ret_w_in[j], ret_w_out[j])
        x = x + mix
        x = x + hierarchical_moe(rms_norm(x, norm_ffn[i]), moe_w_group[i], moe_b_group[i],
                                 moe_w_expert[i], moe_b_expert[i], moe_w_gate[i],
                                 moe_w_up[i], moe_w_down[i])
    return rms_norm(x, norm_final)


_drawn_inputs = setup_inputs


def setup_inputs(seed=0):
    import zlib

    import numpy as np

    out = dict(_drawn_inputs(seed))
    spreads = {}
    factors = {'norm_mix': 3.012,
     'norm_ffn': 3.744,
     'norm_final': 5.755,
     'diff_subln': 3.761,
     'moe_b_group': 7.57,
     'moe_b_expert': 4.816}
    for name, (base, spread) in spreads.items():
        noise = np.random.default_rng([zlib.crc32(name.encode()), seed]).standard_normal(out[name].shape)
        drawn = base * np.exp(spread * noise) if base else spread * noise
        out[name] = jnp.asarray(drawn.astype(out[name].dtype))
    for name, factor in factors.items():
        out[name] = (out[name] * factor).astype(out[name].dtype)
    return out
```

```python
from contextlib import ExitStack

import concourse.bass as bass
from concourse import mybir

F32 = mybir.dt.float32
F32R = mybir.dt.float32r
I32 = mybir.dt.int32
U32 = mybir.dt.uint32
ALU = mybir.AluOpType
ACT = mybir.ActivationFunctionType
AX = mybir.AxisListType

P = 128
SEQ = 2048
D = 1024
TILES = SEQ // P
KC = D // P
HEADS = 8
HALF = 64
NEG = -1e30
LOWEST = -3e38
LAMBDA_INIT = 0.8 - 0.6
POOL_NOT = 50


def gate(eng, sem, value, passed):
    eng.wait_ge(sem, value)
    eng.sem_inc(passed, 1)


def project(nc, io, keep, scratch, sem):
    GROUPS = SEQ // 512
    WB = 256
    QKB = 2 * D // WB
    VB = D // WB
    BLOCKS = QKB + VB
    x_rows = io["x"].rearrange("o (t p) d -> (o t) p d", p=P)
    w_rows = io["diff_w_in"].rearrange("o (c p) n -> p (o c) n", p=P)
    with ExitStack() as ctx:
        def sb(name, shape, dt=F32):
            return ctx.enter_context(nc.sbuf_tensor(name, shape, dt))

        hnT_hi = sb("hnT_hi", [P, KC, SEQ], F32R)
        hnT_lo = sb("hnT_lo", [P, KC, SEQ], F32R)
        w_raw = sb("w_raw", [P, KC, WB])
        w_hi = sb("w_hi", [P, 2, KC, WB], F32R)
        w_lo = sb("w_lo", [P, 2, KC, WB], F32R)
        stage = sb("stage", [P, 4, 2 * 512], F32R)
        g_row = sb("g_row", [P, D])
        xt = sb("xt", [P, 4, D])
        sumsq = sb("sumsq", [P, 4])
        root = sb("root", [P, 4])
        rstd = sb("rstd", [P, 4])
        eps = sb("eps", [P, 1])
        ps = ctx.enter_context(nc.psum_tensor("ps1", [P, 8, 512], F32))
        ident = keep["ident"]
        s = lambda name: sem("a_" + name)
        x_in = [s(f"x_in{i}") for i in range(4)]
        g_in, eps_set, w_in, w_split = s("g_in"), s("eps_set"), s("w_in"), s("w_split")
        squared, rooted, inverted, normed = s("squared"), s("rooted"), s("inverted"), s("normed")
        turned, hn_hi, hn_lo = s("turned"), s("hn_hi"), s("hn_lo")
        filled, out_hi, out_lo, w_hi_set = s("filled"), s("out_hi"), s("out_lo"), s("w_hi_set")
        stored = [s(f"stored{i}") for i in range(4)]
        passed = sem("passed")
        ident_set = keep["ident_set"]
        block = ctx.enter_context(nc.Block())
        BANKS = 8
        QK_FILLS = QKB * BANKS
        V_FILLS = VB * TILES

        @block.sync
        def _(sp):
            sp.dma_start(g_row[:, :], io["norm_mix"].to_broadcast([P, D])).then_inc(g_in, 16)
            with sp.Fori(0, GROUPS) as g:
                for i in range(4):
                    sp.wait_ge(turned, g * 4 + i + 1)
                    sp.dma_start(xt[:, i, :], x_rows[bass.ds(g * 4 + i, 1)].rearrange("o p d -> (o p) d")
                                 ).then_inc(x_in[i], 16)
            with sp.Fori(0, QKB) as b:
                for n in range(8):
                    sp.wait_ge(out_lo, b * 8 + (BANKS + n + 1))
                    dst = scratch["qk"][bass.ds(b * 2 + n // 4, 1)].rearrange("o h p t -> p (o h) t")
                    sp.dma_start(dst[:, :, (n % 4) * 512:(n % 4) * 512 + 512],
                                 stage[:, n % 4, :].bitcast(F32).rearrange("p (h t) -> p h t", h=2)).then_inc(stored[n % 4], 16)
            with sp.Fori(0, VB) as b:
                for n in range(TILES):
                    sp.wait_ge(out_lo, b * TILES + (BANKS + QK_FILLS + n + 1))
                    dst = scratch["v"][bass.ds(b * 2, 2), n].rearrange("h p e -> p h e")
                    sp.dma_start(dst, stage[:, n % 4, 0:512].bitcast(F32).rearrange("p (h e) -> p h e", h=2)
                                 ).then_inc(stored[n % 4], 16)
            for i in range(4):
                sp.wait_ge(stored[i], 16 * (QK_FILLS + V_FILLS) // 4 + 1)

        @block.gpsimd
        def _(pool):
            pool.memset(ident[:, :], 1.0).then_inc(ident_set, 1)
            pool.wait_ge(ident_set, 1)
            pool.affine_select(out=ident[:, :], in_=ident[:, :], compare_op=ALU.is_equal, fill=0.0, base=0,
                               pattern=[[-1, P]], channel_multiplier=1).then_inc(ident_set, 1)
            pool.memset(eps[:, :], 1e-6).then_inc(eps_set, 1)
            with pool.Fori(0, BLOCKS) as b:
                gate(pool, w_split, b + 1, passed)
                pool.dma_start(w_raw[:, :, :], w_rows[:, :, bass.ds(b * WB, WB)]).then_inc(w_in, 16)

        @block.scalar
        def _(act):
            act.sem_inc(squared, 1)
            act.wait_ge(eps_set, 1)
            with act.Fori(0, GROUPS) as g:
                for i in range(4):
                    act.wait_ge(x_in[i], g * 16 + 16)
                    act.wait_ge(squared, g * 4 + (i + 1))
                    nc.scalar.activation(ps[:, 6:8, :].rearrange("p a b -> p (a b)"), xt[:, i, :], ACT.Square,
                                         accum_out=sumsq[:, i:i + 1]).then_inc(squared, 1)
                act.wait_ge(squared, g * 4 + 5)
                act.wait_ge(inverted, g + 1)
                nc.scalar.activation(root[:, :], sumsq[:, :], ACT.Sqrt, bias=eps[:, 0:1], scale=1.0 / D).then_inc(rooted, 1)
                for i in range(4):
                    act.wait_ge(turned, g * 4 + i + 5)
                    src = ps[:, (i % 2) * 2:(i % 2) * 2 + 2, :].rearrange("p a (b t) -> p (a b) t", t=P)
                    nc.scalar.activation(hnT_hi[:, :, bass.ds(g * 512 + i * P, P)], src, ACT.Copy).then_inc(hn_hi, 1)

            def take(fill, n, slot_uses, dst, src):
                act.wait_ge(filled, fill + 1)
                act.wait_ge(stored[n % 4], slot_uses + 1)
                nc.scalar.activation(dst, src, ACT.Copy).then_inc(out_hi, 1)

            with act.Fori(0, QKB) as b:
                for n in range(8):
                    take(b * 8 + n + 1, n, b * 32 + 16 * (n // 4), stage[:, n % 4, 0:512], ps[:, n, :])
            with act.Fori(0, VB) as b:
                for n in range(TILES):
                    take(b * TILES + (QK_FILLS + n + 1), n, b * 64 + (QKB * 32 + 16 * (n // 4)),
                         stage[:, n % 4, 0:512].rearrange("p (h e) -> p h e", h=2)[:, :, 0:P],
                         ps[:, n % 8, 0:WB].rearrange("p (h e) -> p h e", h=2))

        @block.vector
        def _(dve):
            dve.sem_inc(out_lo, BANKS)
            dve.sem_inc(hn_lo, 2)
            for one in [w_split, inverted, normed, *stored]:
                dve.sem_inc(one, 1)
            dve.wait_ge(g_in, 16)
            with dve.Fori(0, GROUPS) as g:
                dve.wait_ge(rooted, g + 1)
                dve.wait_ge(normed, g * 4 + 1)
                nc.vector.reciprocal(rstd[:, :], root[:, :]).then_inc(inverted, 1)
                dve.wait_ge(inverted, g + 2)
                for i in range(4):
                    nc.vector.scalar_tensor_tensor(out=xt[:, i, :], in0=xt[:, i, :], scalar=rstd[:, i:i + 1],
                                                   in1=g_row[:, :], op0=ALU.mult, op1=ALU.mult).then_inc(normed, 1)
                for i in range(4):
                    dve.wait_ge(hn_hi, g * 4 + i + 1)
                    src = ps[:, (i % 2) * 2:(i % 2) * 2 + 2, :].rearrange("p a (b t) -> p (a b) t", t=P)
                    nc.vector.tensor_tensor(hnT_lo[:, :, bass.ds(g * 512 + i * P, P)], src,
                                            hnT_hi[:, :, bass.ds(g * 512 + i * P, P)].bitcast(F32),
                                            ALU.subtract).then_inc(hn_lo, 1)

            def split(b, slot, freed=None):
                dve.wait_ge(w_in, b * 16 + 16)
                if freed is not None:
                    dve.wait_ge(filled, freed + 1)
                nc.vector.tensor_copy(w_hi[:, slot], w_raw[:, :, :]).then_inc(w_hi_set, 1)
                dve.wait_ge(w_hi_set, b + 1)
                nc.vector.tensor_tensor(w_lo[:, slot], w_raw[:, :, :], w_hi[:, slot].bitcast(F32),
                                        ALU.subtract).then_inc(w_split, 1)

            def take(fill, dst, hi, src):
                dve.wait_ge(out_hi, fill)
                nc.vector.tensor_tensor(dst, src, hi.bitcast(F32), ALU.subtract).then_inc(out_lo, 1)

            split(0, 0)
            with dve.Fori(0, QKB // 2) as b2:
                for half in range(2):
                    split(b2 * 2 + half + 1, 1 - half, b2 * 16 + half * 8)
                    for n in range(8):
                        take(b2 * 16 + half * 8 + n + 1, stage[:, n % 4, 512:1024], stage[:, n % 4, 0:512], ps[:, n, :])
            for b in range(VB):
                if b + 1 < VB:
                    split(QKB + b + 1, (b + 1) % 2, QK_FILLS + b * TILES)
                for n in range(TILES):
                    out = stage[:, n % 4, 0:512].rearrange("p (h e) -> p h e", h=2)
                    take(QK_FILLS + b * TILES + n + 1, out[:, :, P:2 * P], out[:, :, 0:P],
                         ps[:, n % 8, 0:WB].rearrange("p (h e) -> p h e", h=2))

        @block.tensor
        def _(pe):
            pe.wait_ge(ident_set, 2)
            pe.sem_inc(turned, 4)
            pe.sem_inc(filled, 1)
            with pe.Fori(0, GROUPS) as g:
                for i in range(4):
                    pe.wait_ge(normed, g * 4 + i + 2)
                    pe.wait_ge(hn_lo, g * 4 + i + 1)
                    for c in range(KC):
                        mm = pe.transpose(ps[:, (i % 2) * 2 + c // 4, (c % 4) * P:(c % 4 + 1) * P],
                                          xt[:, i, c * P:(c + 1) * P], ident[:, :])
                    mm.then_inc(turned, 1)

            TERMS = ((w_lo, hnT_hi), (w_hi, hnT_lo), (w_hi, hnT_hi))
            pe.wait_ge(hn_lo, TILES + 2)
            with pe.Fori(0, QKB // 2) as b2:
                for half in range(2):
                    pe.wait_ge(w_split, b2 * 2 + (half + 2))
                    for n in range(8):
                        pe.wait_ge(out_lo, b2 * 16 + (half * 8 + n + 1))
                        k = 0
                        for w, h in TERMS:
                            for c in range(KC):
                                mm = pe.matmul(ps[:, n, :], w[:, half, c, (n // 4) * P:(n // 4 + 1) * P],
                                               h[:, c, (n % 4) * 512:(n % 4 + 1) * 512], start=k == 0, stop=k == 23)
                                k += 1
                        mm.then_inc(filled, 1)
            with pe.Fori(0, VB // 2) as b2:
                for half in range(2):
                    pe.wait_ge(w_split, b2 * 2 + (QKB + half + 2))
                    for n in range(TILES):
                        pe.wait_ge(out_lo, b2 * (2 * TILES) + (QK_FILLS + half * TILES + n + 1))
                        k = 0
                        for w, h in TERMS:
                            for c in range(KC):
                                mm = pe.matmul(ps[:, n % 8, 0:WB], h[:, c, n * P:(n + 1) * P], w[:, half, c, :],
                                               start=k == 0, stop=k == 23)
                                k += 1
                        mm.then_inc(filled, 1)


def attend(nc, io, keep, scratch, sem):
    ROWS = [1, 3, 5, 7, 9, 11, 13, 15, 14, 12, 10, 8, 6, 4, 2, 0]
    SCALE = HALF ** -0.5
    NEAR = 2 * P
    WIDE = 1024
    PAIRS = HEADS // 2
    RING = 4
    AHEAD = RING - 1
    Q_RING = 4

    def pieces(i):
        w = (i + 1) * P
        return [(0, w)] if w <= WIDE else [(0, w - WIDE), (w - WIDE, WIDE)]

    rows = [(half, i) for half in range(2) for i in ROWS]
    NR = len(rows)
    chunks, groups, parts, n_c, n_g, n_r = [], [], [], 0, 0, [0]
    for half, i in rows:
        cs = []
        for m in range(2):
            for k0, w in pieces(i):
                cs.append((n_c, m, k0, w))
                n_c += 1
        gs = []
        for g in range(i // 4 + 1):
            gs.append((n_g, 4 * g, min(4 * g + 4, i + 1)))
            n_g += 1
        chunks.append(cs)
        parts.append([(m, k0, min(WIDE, (i + 1) * P - k0)) for m in range(2) for k0 in range(0, (i + 1) * P, WIDE)])
        n_r.append(n_r[-1] + len(parts[-1]))
        groups.append(gs)
    shared = [r for r, (_, i) in enumerate(rows) if i >= 2]
    NS = len(shared)

    def cut(i):
        return (i + 1) * P if i < 2 else ((i + 1) * POOL_NOT) // 100 * P + (P if ((i + 1) * POOL_NOT) % 100 else 0)

    def order(r):
        a = [("S", c) for c in chunks[r + AHEAD]] if r + AHEAD < NR else []
        b = []
        if r >= 0:
            gs = groups[r]
            for k, g in enumerate(gs):
                b.append(("T", g))
                if k:
                    b.append(("V", gs[k - 1]))
            b.append(("V", gs[-1]))
        out = []
        while a or b:
            if a:
                out.append(a.pop(0))
            if b:
                out.append(b.pop(0))
            if len(b) > 2 * len(a) and b:
                out.append(b.pop(0))
        return out

    with ExitStack() as ctx:
        def sb(name, shape, dt=F32):
            return ctx.enter_context(nc.sbuf_tensor(name, shape, dt))

        q_st = sb("q_st", [P, Q_RING, 2, P], F32R)
        k_hi = sb("k_hi", [P, 2, 2, SEQ], F32R)
        k_lo = sb("k_lo", [P, 2, 2, SEQ], F32R)
        v_hl = sb("v_hl", [P, 2, TILES, 2 * P], F32R)
        near = sb("near", [P, 2, NEAR])
        prob = sb("prob", [P, RING, 2, SEQ])
        aT_hi = sb("aT_hi", [P, 4, 512], F32R)
        aT_lo = sb("aT_lo", [P, 4, 512], F32R)
        top = sb("top", [P, 2, 2, 3])
        peak = sb("peak", [P, 2, 2])
        shift = sb("shift", [P, 4, 2])
        sums = sb("sums", [P, 4, 2, 2])
        total = sb("total", [P, 4, 2])
        inv = sb("inv", [P, 4, 2])
        coef = sb("coef", [P, 4, 1])
        part = sb("part", [P, 2, P])
        o_sb = sb("o_sb", [P, 2, P])
        lq = sb("lq", [P, 4, HALF])
        dots = sb("dots", [P, 2])
        edots = sb("edots", [P, 2])
        neg_lam = sb("neg_lam", [P, 1])
        flip = sb("flip", [P, P])
        z = sb("z", [HEADS, 3 * P])
        z0 = sb("z0", [HEADS, 1])
        onehot = sb("onehot", [32, 3 * P])
        table = sb("table", [32, HEADS])
        ps_s = ctx.enter_context(nc.psum_tensor("ps_s", [P, 2, WIDE], F32))
        ps_t = ctx.enter_context(nc.psum_tensor("ps_t", [P, 2, 512], F32))
        ps_o = ctx.enter_context(nc.psum_tensor("ps_o", [P, 2, 512], F32))
        ident = keep["ident"]
        s = lambda name: sem("b_" + name)
        head_in = [s("head_in0"), s("head_in1")]
        scored, taken, shifted, raised = s("scored"), s("taken"), s("shifted"), s("raised")
        peaked, inverted, coefed = s("peaked"), s("inverted"), s("coefed")
        q_in = [s(f"q_in{k}") for k in range(Q_RING)]
        scaled, mixed_v, mixed_p = s("scaled"), s("mixed_v"), s("mixed_p")
        turned, t_hi, t_lo, summed = s("turned"), s("t_hi"), s("t_lo"), s("summed")
        parted, o_set = s("parted"), s("o_set")
        o_out = [s("o_out0"), s("o_out1")]
        tab_in, z_set, moved, flipped, near_set = (
            s("tab_in"), s("z_set"), s("moved"), s("flipped"), s("near_set"))
        lq_in, dotted, lam_set, flip_set = s("lq_in"), s("dotted"), s("lam_set"), s("flip_set")
        passed = sem("passed")
        block = ctx.enter_context(nc.Block())
        TAKEN0, TURNED0, T_LO0, SUMMED0, O_SET0, O_OUT0, PARTED0 = 2, 1, 2, 4, 2, 1, 1
        skewed, unskewed = prob[:, 2, 0, :], prob[:, 2, 1, :]

        @block.sync
        def _(sp):
            sp.dma_start(table[:, :], io["rel_bias_table"]).then_inc(tab_in, 16)
            sp.dma_start(onehot[:, :], io["bucket_of_distance"]).then_inc(tab_in, 16)
            sp.dma_start(lq[:, :, :], io["diff_lambda_qk"].rearrange("o a d -> o (a d)").to_broadcast([P, 4 * HALF])
                         .rearrange("p (a d) -> p a d", a=4)).then_inc(lq_in, 16)

            qk = scratch["qk"]

            def load(h, buf):
                sm = head_in[buf]
                for m in range(2):
                    for k_op, hl in ((k_hi, 0), (k_lo, 1)):
                        for lanes in (slice(0, HALF), slice(HALF, P)):
                            sp.dma_start(k_op[lanes, buf, m, :].bitcast(F32),
                                         qk[bass.ds(h + HEADS, 1), hl, m * HALF:(m + 1) * HALF, :]
                                         .rearrange("o p t -> (o p) t")).then_inc(sm, 16)
                sp.dma_start(v_hl[:, buf].bitcast(F32),
                             scratch["v"][bass.ds(h, 1)].rearrange("o t p e -> p (o t) e")).then_inc(sm, 16)
                sp.dma_start(near[:, buf, :], scratch["near"][bass.ds(h, 1)].rearrange("o p c -> (o p) c")).then_inc(sm, 16)

            def load_q(it, r):
                half, i = rows[r]
                done = chunks[r - Q_RING][-1][0] + 1 if r >= Q_RING else 0
                gate(sp, taken, it * n_c + (done + TAKEN0), passed)
                for hl in range(2):
                    sp.dma_start(q_st[hl * HALF:(hl + 1) * HALF, r % Q_RING, :, :].bitcast(F32),
                                 qk[bass.ds(it * 2 + half, 1), hl, :, i * P:(i + 1) * P]
                                 .rearrange("o (m d) t -> d (o m) t", m=2)).then_inc(q_in[r % Q_RING], 16)

            sp.wait_ge(z_set, 3)
            sp.dma_start(scratch["z"], z[:, :]).then_inc(moved, 16)
            sp.wait_ge(moved, 16)
            zt = scratch["z"]
            sp.dma_start(skewed.rearrange("p (h c) -> p h c", h=HEADS),
                         bass.AP(tensor=zt.tensor, offset=0, ap=[[1, P], [3 * P, HEADS], [1, NEAR]])).then_inc(tab_in, 16)
            sp.wait_ge(near_set, 4)
            sp.dma_start(scratch["near"].rearrange("h p c -> p h c"),
                         unskewed.rearrange("p (h c) -> p h c", h=HEADS)).then_inc(moved, 16)
            sp.wait_ge(moved, 32)
            load(0, 0)

            def pair(it, more):
                for r in range(NR):
                    load_q(it, r)
                    if r == 5:
                        gate(sp, summed, it * n_g + SUMMED0, passed)
                        load(it * 2 + 1, 1)
                    if r == TILES + 5 and more:
                        gate(sp, summed, it * n_g + (groups[TILES - 1][-1][0] + 1 + SUMMED0), passed)
                        load(it * 2 + 2, 0)

            with sp.Fori(0, PAIRS - 1) as it:
                pair(it, True)
            pair(PAIRS - 1, False)

        @block.gpsimd
        def _(pool):
            pool.memset(flip[:, :], 1.0).then_inc(flip_set, 1)
            pool.wait_ge(flip_set, 1)
            pool.affine_select(out=flip[:, :], in_=flip[:, :], compare_op=ALU.is_equal, fill=0.0, base=-(P - 1),
                               pattern=[[1, P]], channel_multiplier=1).then_inc(flip_set, 1)
            with pool.Fori(0, PAIRS) as it:
                for n, r in enumerate(shared):
                    i = rows[r][1]
                    x, w = cut(i), (i + 1) * P
                    p0, p1 = prob[:, r % RING, 0, x:w], prob[:, r % RING, 1, x:w]
                    gate(pool, coefed, it * NR + (r + 1), passed)
                    pool.tensor_scalar(p1, p1, coef[:, r % 4, :], 0.0, ALU.mult, ALU.add).then_inc(scaled, 1)
                    pool.wait_ge(scaled, it * NS + (n + 1))
                    pool.tensor_tensor(p0, p0, p1, ALU.add).then_inc(mixed_p, 1)

        @block.scalar
        def _(act):
            act.wait_ge(dotted, 2)
            nc.scalar.activation(edots[:, :], dots[:, :], ACT.Exp).then_inc(lam_set, 1)

            def raise_(it, r, m, k0, w):
                if m == 0 and k0 == 0:
                    act.wait_ge(shifted, it * NR + (r + 1))
                nc.scalar.activation(prob[:, r % RING, m, k0:k0 + w], prob[:, r % RING, m, k0:k0 + w], ACT.Exp,
                                     bias=shift[:, r % 4, m:m + 1], scale=SCALE,
                                     accum_out=sums[:, r % 4, m, (1 if k0 else 0):(2 if k0 else 1)]).then_inc(raised, 1)

            def store(it, r):
                half, i = rows[r]
                act.wait_ge(o_set, it * NR + (r + 1 + O_SET0))
                act.dma_start(scratch["o"][i * P:(i + 1) * P, bass.ds((it * 2 + half) * P, P)],
                              o_sb[:, r % 2, :]).then_inc(o_out[r % 2], 16)

            def out(it, r):
                act.wait_ge(summed, it * n_g + (groups[r][-1][0] + 1 + SUMMED0))
                act.wait_ge(o_set, it * NR + (r - 1 + O_SET0))
                nc.scalar.activation(part[:, r % 2, :], ps_o[:, r % 2, P:2 * P], ACT.Copy,
                                     scale=inv[:, r % 4, 0:1]).then_inc(parted, 1)

            with act.Fori(0, PAIRS) as it:
                for r in range(-AHEAD, NR):
                    if r - 1 >= 0:
                        out(it, r - 1)
                    waiting = list(parts[r + 2]) if 0 <= r + 2 < NR else []
                    turns = [what for kind, what in order(r) if kind == "T"]
                    for n_t, (g, k0, k1) in enumerate(turns):
                        act.wait_ge(turned, it * n_g + (g + 1 + TURNED0))
                        act.wait_ge(summed, it * n_g + (g - 3 + SUMMED0))
                        n = (k1 - k0) * P
                        nc.scalar.activation(aT_hi[:, g % 4, 0:n], ps_t[:, g % 2, 0:n], ACT.Copy).then_inc(t_hi, 1)
                        while waiting and len(waiting) * len(turns) > (len(turns) - n_t - 1) * len(parts[r + 2]):
                            raise_(it, r + 2, *waiting.pop(0))
                    for what in waiting:
                        raise_(it, r + 2, *what)
                    if r - 1 >= 0:
                        store(it, r - 1)
                out(it, NR - 1)
                store(it, NR - 1)
            for k in range(2):
                act.wait_ge(o_out[k], 16 * PAIRS * NR // 2 + O_OUT0)

        @block.vector
        def _(dve):
            dve.sem_inc(taken, TAKEN0)
            dve.sem_inc(t_lo, T_LO0)
            dve.sem_inc(o_set, O_SET0)
            dve.wait_ge(flipped, 1)
            nc.vector.tensor_copy(z0[:, :], ps_t[0:HEADS, 0, 0:1]).then_inc(z_set, 1)
            dve.wait_ge(z_set, 1)
            nc.vector.tensor_scalar(z[:, :], ps_t[0:HEADS, 0, 0:3 * P], z0[:, 0:1], 1.0 / SCALE,
                                    ALU.subtract, ALU.mult).then_inc(z_set, 1)
            dve.wait_ge(z_set, 2)
            nc.vector.memset(z[:, NEAR:3 * P], NEG).then_inc(z_set, 1)
            dve.wait_ge(lq_in, 16)
            for k in range(2):
                nc.vector.tensor_tensor_reduce(lq[:, 2 * k, :], lq[:, 2 * k, :], lq[:, 2 * k + 1, :], 1.0, 0.0,
                                               ALU.mult, ALU.add, dots[:, k:k + 1]).then_inc(dotted, 1)
            dve.wait_ge(lam_set, 1)
            nc.vector.scalar_tensor_tensor(out=neg_lam[:, :], in0=edots[:, 1:2], scalar=LAMBDA_INIT,
                                           in1=edots[:, 0:1], op0=ALU.subtract, op1=ALU.subtract).then_inc(lam_set, 1)
            dve.wait_ge(flipped, 2)
            for k in range(4):
                nc.vector.tensor_copy(unskewed[:, k * 512:(k + 1) * 512],
                                      ps_s[:, k // 2, (k % 2) * 512:(k % 2 + 1) * 512]).then_inc(near_set, 1)
            dve.wait_ge(lam_set, 2)

            def take(it, r, c, m, k0, w):
                half, i = rows[r]
                last = k0 + w == (i + 1) * P
                n_near = min(w, NEAR) if last else 0
                far = w - n_near
                if m == 0 and k0 == 0 and r >= RING:
                    dve.wait_ge(turned, it * n_g + (groups[r - RING][-1][0] + 1 + TURNED0))
                elif m == 0 and k0 == 0:
                    dve.wait_ge(turned, it * n_g + TURNED0)
                if far:
                    dve.wait_ge(scored, it * n_c + (c + 1))
                    col = 0 if not last else 1
                    ins = nc.vector.tensor_scalar(prob[:, r % RING, m, k0:k0 + far], ps_s[:, c % 2, 0:far], 1.0, None,
                                                  ALU.mult, ALU.max, accum_out=top[:, r % 2, m, col:col + 1])
                else:
                    gate(dve, scored, it * n_c + (c + 1), passed)
                if n_near:
                    ins = nc.vector.tensor_tensor_reduce(
                        prob[:, r % RING, m, k0 + far:k0 + w], ps_s[:, c % 2, far:w], near[:, half, NEAR - n_near:NEAR],
                        1.0, LOWEST, ALU.add, ALU.max, top[:, r % 2, m, 2:3])
                ins.then_inc(taken, 1)

            def peaks(it, r):
                i = rows[r][1]
                first = 0 if i >= 8 else 1 if i >= 2 else 2
                dve.wait_ge(taken, it * n_c + (chunks[r][-1][0] + 1 + TAKEN0))
                nc.vector.tensor_reduce(peak[:, r % 2, :], top[:, r % 2, :, first:3], AX.X, ALU.max).then_inc(peaked, 1)
                dve.wait_ge(peaked, it * NR + (r + 1))
                nc.vector.tensor_scalar(shift[:, r % 4, :], peak[:, r % 2, :], -SCALE, None, ALU.mult).then_inc(shifted, 1)

            def mix(it, r):
                i = rows[r][1]
                if i >= 8:
                    dve.wait_ge(raised, it * n_r[-1] + n_r[r + 1])
                    nc.vector.tensor_reduce(total[:, r % 4, :], sums[:, r % 4, :, :], AX.X, ALU.add).then_inc(inverted, 1)
                else:
                    dve.wait_ge(raised, it * n_r[-1] + n_r[r + 1])
                    nc.vector.tensor_copy(total[:, r % 4, :], sums[:, r % 4, :, 0]).then_inc(inverted, 1)
                dve.wait_ge(inverted, it * (2 * NR) + (2 * r + 1))
                nc.vector.reciprocal(inv[:, r % 4, :], total[:, r % 4, :]).then_inc(inverted, 1)
                dve.wait_ge(inverted, it * (2 * NR) + (2 * r + 2))
                nc.vector.scalar_tensor_tensor(out=coef[:, r % 4, :], in0=total[:, r % 4, 0:1], scalar=neg_lam[:, 0:1],
                                               in1=inv[:, r % 4, 1:2], op0=ALU.mult, op1=ALU.mult).then_inc(coefed, 1)
                dve.wait_ge(coefed, it * NR + (r + 1))
                x = cut(i)
                p0, p1 = prob[:, r % RING, 0, 0:x], prob[:, r % RING, 1, 0:x]
                nc.vector.scalar_tensor_tensor(out=p0, in0=p1, scalar=coef[:, r % 4, :], in1=p0,
                                               op0=ALU.mult, op1=ALU.add).then_inc(mixed_v, 1)

            def out(it, r):
                dve.wait_ge(parted, it * NR + (r + 1))
                dve.wait_ge(o_out[r % 2], it * (16 * NR // 2) + (16 * (r // 2) + O_OUT0))
                nc.vector.scalar_tensor_tensor(out=o_sb[:, r % 2, :], in0=ps_o[:, r % 2, 0:P], scalar=inv[:, r % 4, 0:1],
                                               in1=part[:, r % 2, :], op0=ALU.mult, op1=ALU.add).then_inc(o_set, 1)

            for k in range(2):
                dve.sem_inc(o_out[k], O_OUT0)
            with dve.Fori(0, PAIRS) as it:
                for r in range(-AHEAD, NR):
                    if 0 <= r + 1 < NR:
                        mix(it, r + 1)
                    if r - 1 >= 0:
                        out(it, r - 1)
                    for kind, what in order(r):
                        if kind == "S":
                            if what is chunks[r + AHEAD][0] and (r + AHEAD) % TILES == 0:
                                dve.wait_ge(head_in[(r + AHEAD) // TILES], it * (16 * 10) + 16 * 10)
                            take(it, r + AHEAD, *what)
                        elif kind == "T":
                            g, k0, k1 = what
                            n = (k1 - k0) * P
                            dve.wait_ge(t_hi, it * n_g + (g + 1))
                            nc.vector.tensor_tensor(aT_lo[:, g % 4, 0:n], ps_t[:, g % 2, 0:n],
                                                    aT_hi[:, g % 4, 0:n].bitcast(F32), ALU.subtract).then_inc(t_lo, 1)
                    if r + AHEAD < NR:
                        peaks(it, r + AHEAD)
                out(it, NR - 1)

        @block.tensor
        def _(pe):
            pe.sem_inc(turned, TURNED0)
            pe.sem_inc(summed, SUMMED0)
            pe.wait_ge(tab_in, 32)
            pe.matmul(ps_t[0:HEADS, 0, 0:3 * P], table[:, :], onehot[:, :], start=True, stop=True).then_inc(flipped, 1)
            pe.wait_ge(tab_in, 48)
            pe.wait_ge(flip_set, 2)
            for k in range(4):
                mm = pe.matmul(ps_s[:, k // 2, (k % 2) * 512:(k % 2 + 1) * 512], flip[:, :],
                               skewed[:, k * 512:(k + 1) * 512], start=True, stop=True)
            mm.then_inc(flipped, 1)
            pe.wait_ge(near_set, 4)
            with pe.Fori(0, PAIRS) as it:
                for r in range(-AHEAD, NR):
                    for kind, what in order(r):
                        if kind == "S":
                            c, m, k0, w = what
                            x = r + AHEAD
                            half, i = rows[x]
                            if what is chunks[x][0] and x % TILES == 0:
                                pe.wait_ge(head_in[half], it * (16 * 10) + 16 * 10)
                            if what is chunks[x][0]:
                                pe.wait_ge(q_in[x % Q_RING], it * (32 * NR // Q_RING) + 32 * (x // Q_RING + 1))
                            pe.wait_ge(taken, it * n_c + (c - 1 + TAKEN0))
                            for j in range(0, w, 512):
                                n = min(512, w - j)
                                for k_op in (k_lo, k_hi):
                                    mm = pe.matmul(ps_s[:, c % 2, j:j + n], q_st[:, x % Q_RING, m, :],
                                                   k_op[:, half, m, k0 + j:k0 + j + n], start=k_op is k_lo,
                                                   stop=k_op is k_hi)
                            mm.then_inc(scored, 1)
                        elif kind == "T":
                            g, k0, k1 = what
                            if k0 == 0:
                                pe.wait_ge(mixed_v, it * NR + (r + 1))
                                if r in shared:
                                    pe.wait_ge(mixed_p, it * NS + (shared.index(r) + 1))
                            pe.wait_ge(t_lo, it * n_g + (g - 1 + T_LO0))
                            for k in range(k0, k1):
                                mm = pe.transpose(ps_t[:, g % 2, (k - k0) * P:(k - k0 + 1) * P],
                                                  prob[:, r % RING, 0, k * P:(k + 1) * P], ident[:, :])
                            mm.then_inc(turned, 1)
                        else:
                            g, k0, k1 = what
                            half, i = rows[r]
                            pe.wait_ge(t_lo, it * n_g + (g + 1 + T_LO0))
                            if k0 == 0:
                                pe.wait_ge(o_set, it * NR + (r - 1 + O_SET0))
                            for k in range(k0, k1):
                                t = slice((k - k0) * P, (k - k0 + 1) * P)
                                pe.matmul(ps_o[:, r % 2, 0:2 * P], aT_hi[:, g % 4, t], v_hl[:, half, k, :],
                                          start=k == 0, stop=False)
                                mm = pe.matmul(ps_o[:, r % 2, 0:P], aT_lo[:, g % 4, t], v_hl[:, half, k, 0:P],
                                               start=False, stop=k == i)
                            mm.then_inc(summed, 1)


EXPERTS = 32
GROUPS_E = 4
PER_GROUP = EXPERTS // GROUPS_E
FF = 512
FC = FF // P
ROUTES = GROUPS_E + EXPERTS
SLOTS = EXPERTS * SEQ + P
BLOCKS_MAX = 2 * SEQ // P + EXPERTS


def mix_and_route(nc, io, keep, scratch, sem):
    with ExitStack() as ctx:
        def sb(name, shape, dt=F32):
            return ctx.enter_context(nc.sbuf_tensor(name, shape, dt))

        wo_raw = sb("wo_raw", [P, KC, D])
        wo_hi = sb("wo_hi", [P, KC, D], F32R)
        wo_lo = sb("wo_lo", [P, KC, D], F32R)
        o_t = sb("o_t", [P, 2, D])
        sq = sb("sq", [P, D])
        sq2 = sb("sq2", [P, D])
        oT_hi = sb("oT_hi", [P, 2, D], F32R)
        oT_lo = sb("oT_lo", [P, 2, D], F32R)
        x2 = sb("x2", [P, 2, D])
        h2 = sb("h2", [P, 2, D])
        h2T = sb("h2T", [P, D])
        g2_row = sb("g2_row", [P, D])
        w_r = sb("w_r", [P, KC, ROUTES])
        b_r = sb("b_r", [P, ROUTES])
        sub_g = sb("sub_g", [P, 1])
        sub_gs = sb("sub_gs", [P, 1])
        eps5, eps6 = sb("eps5", [P, 1]), sb("eps6", [P, 1])
        ssh, rth, rih = sb("ssh", [P, HEADS]), sb("rth", [P, HEADS]), sb("rih", [P, HEADS])
        ss2, rt2, ri2 = sb("ss2", [P, 1]), sb("rt2", [P, 1]), sb("ri2", [P, 1])
        lg = sb("lg", [P, 8])
        le = sb("le", [P, EXPERTS])
        gm, gi = sb("gm", [P, 8]), sb("gi", [P, 8], U32)
        gf, g8 = sb("gf", [P, 1]), sb("g8", [P, 1])
        gmask = sb("gmask", [P, GROUPS_E])
        em = sb("em", [P, EXPERTS])
        es = sb("es", [P, PER_GROUP])
        ev, ei = sb("ev", [P, 8]), sb("ei", [P, 8], U32)
        ef = sb("ef", [P, 2])
        eid = sb("eid", [P, 2, 2])
        own = sb("own", [P, 2, 2, EXPERTS])
        both = sb("both", [P, 2, EXPERTS])
        before = sb("before", [P, EXPERTS])
        rank = sb("rank", [P, 2, 2])
        junk = sb("junk", [P, 2, EXPERTS])
        slot_f, slot = sb("slot_f", [P, 2]), sb("slot", [P, 2, 2], I32)
        tok_f, tok = sb("tok_f", [P, 1]), sb("tok", [P, 2], I32)
        iota_e, iota_ef = sb("iota_e", [P, EXPERTS], I32), sb("iota_ef", [P, EXPERTS])
        iota_p, iota_pf = sb("iota_p", [P, 1], I32), sb("iota_pf", [P, 1])
        ones, tri = sb("ones", [P, P]), sb("tri", [P, P])
        zeros = sb("zeros", [P, SLOTS // P], I32)
        cnt_i, nb_i = sb("cnt_i", [P, EXPERTS], I32), sb("nb_i", [P, EXPERTS], I32)
        nb, upto = sb("nb", [P, EXPERTS]), sb("upto", [P, EXPERTS])
        one_e = sb("one_e", [P, EXPERTS])
        cmp = sb("cmp", [P, EXPERTS])
        tabf, tabi = sb("tabf", [P, 8]), sb("tabi", [P, 8], I32)
        ps_a = ctx.enter_context(nc.psum_tensor("ps_a", [P, D], F32))
        ps_b = ctx.enter_context(nc.psum_tensor("ps_b", [P, D], F32))
        ps_c = ctx.enter_context(nc.psum_tensor("ps_c", [P, D], F32))
        ps_d = ctx.enter_context(nc.psum_tensor("ps_d", [P, 512], F32))
        ps_e = ctx.enter_context(nc.psum_tensor("ps_e", [P, 512], F32))
        ident, start, kept, e_all, rank_all = (keep[k] for k in ("ident", "start", "kept", "e_all", "rank_all"))
        s = lambda name: sem("c_" + name)
        wo_in, wo_hi_set, wo_split = s("wo_in"), s("wo_hi_set"), s("wo_split")
        o_in = [s("o_in0"), s("o_in1")]
        x_in = [s("x_in0"), s("x_in1")]
        const_in, made, tri_set, gain_set, index_set = (
            s("const_in"), s("made"), s("tri_set"), s("gain_set"), s("index_set"))
        squared, summed, rooted, inverted, normed = (s(n) for n in ("squared", "summed", "rooted", "inverted", "normed"))
        turned, oT_hi_set, oT_lo_set, projected, x2_set = (s(n) for n in ("turned", "oT_hi", "oT_lo", "projected", "x2"))
        squared2, rooted2, inverted2, h2_set = (s(n) for n in ("squared2", "rooted2", "inverted2", "h2"))
        x2_out, h2_out = [s("x2_out0"), s("x2_out1")], [s("h2_out0"), s("h2_out1")]
        turned2, h2T_set, routed, chosen, both_set = (s(n) for n in ("turned2", "h2T", "routed", "chosen", "both"))
        ranked, placed, slot_set, scattered, zeroed = (s(n) for n in ("ranked", "placed", "slot", "scattered", "zeroed"))
        freed, counted, tabled, tab_set, tab_out = s("freed"), s("counted"), s("tabled"), s("tab_set"), s("tab_out")
        passed = sem("passed")
        block = ctx.enter_context(nc.Block())
        x_rows = io["x"].rearrange("o (t p) d -> (o t) p d", p=P)
        TURNED0, OT_LO0, PROJECTED0, X2_0, H2T0, ROUTED0, BOTH0, SLOT0, SUMMED0 = 2, 1, 2, 1, 1, 1, 1, 1, 1
        OUT0, FREED0, ROOTED2_0 = 1, 2, 1
        DEEP = 5

        def steps(eng, step):
            for n in range(DEEP):
                step(n, n % 2, n)
            pairs = (TILES - 1 - DEEP) // 2
            with eng.Fori(0, pairs) as it:
                for j in range(2):
                    step(it * 2 + (DEEP + j), (DEEP + j) % 2, DEEP)
            for n in range(DEEP + 2 * pairs, TILES + DEEP):
                step(n, n % 2, n)

        def has(at, lag):
            return 0 <= at - lag < TILES

        def uses(t, q):
            return t * 8 - 8 * q if q else t * 8

        def tile_of(dram, t):
            return dram.rearrange("(t p) d -> t p d", p=P)[bass.ds(t, 1)].rearrange("o p d -> (o p) d")

        @block.sync
        def _(sp):
            sp.dma_start(o_t[:, 0, :], tile_of(scratch["o"], 0)).then_inc(o_in[0], 16)
            sp.dma_start(wo_raw[:, :, :], io["diff_w_out"].rearrange("o (c p) n -> p (o c) n", p=P)).then_inc(wo_in, 16)
            sp.dma_start(g2_row[:, :], io["norm_ffn"].to_broadcast([P, D])).then_inc(const_in, 16)
            sp.dma_start(w_r[:, :, 0:GROUPS_E], io["moe_w_group"].rearrange("o (c p) n -> p (o c) n", p=P)).then_inc(const_in, 16)
            sp.dma_start(w_r[:, :, GROUPS_E:], io["moe_w_expert"].rearrange("o (c p) n -> p (o c) n", p=P)).then_inc(const_in, 16)
            sp.dma_start(b_r[:, 0:GROUPS_E], io["moe_b_group"].to_broadcast([P, GROUPS_E])).then_inc(const_in, 16)
            sp.dma_start(b_r[:, GROUPS_E:], io["moe_b_expert"].to_broadcast([P, EXPERTS])).then_inc(const_in, 16)
            sp.dma_start(sub_g[:, :], io["diff_subln"].rearrange("o p -> p o")).then_inc(const_in, 16)

            def step(n, par, at):
                if has(at, -1):
                    gate(sp, turned, n + TURNED0, passed)
                    sp.dma_start(o_t[:, 1 - par, :], tile_of(scratch["o"], n + 1)).then_inc(o_in[1 - par], 16)
                if has(at, 2):
                    t = n - 2
                    gate(sp, h2_set, t + 1, passed)
                    sp.dma_start(tile_of(scratch["x2"], t), x2[:, par, :]).then_inc(x2_out[par], 16)
                    sp.dma_start(tile_of(scratch["h2"], t), h2[:, par, :]).then_inc(h2_out[par], 16)
                if has(at, 0):
                    gate(sp, x2_out[par], uses(n, par) + OUT0, passed)
                    sp.dma_start(x2[:, par, :], x_rows[bass.ds(n, 1)].rearrange("o p d -> (o p) d")).then_inc(x_in[par], 16)

            steps(sp, step)
            for k in range(2):
                sp.wait_ge(x2_out[k], 8 * TILES + OUT0)
                sp.wait_ge(h2_out[k], 8 * TILES + OUT0)
            sp.wait_ge(tab_set, 1)
            sp.dma_start(scratch["tab"], tabi[:, :]).then_inc(tab_out, 16)
            sp.wait_ge(tab_out, 16)

        @block.gpsimd
        def _(pool):
            pool.memset(zeros[:, :], 0).then_inc(made, 1)
            pool.memset(ones[:, :], 1.0).then_inc(made, 1)
            pool.memset(one_e[:, :], 1.0).then_inc(made, 1)
            pool.memset(before[:, :], 0.0).then_inc(made, 1)
            pool.memset(lg[:, :], LOWEST).then_inc(made, 1)
            pool.memset(eps5[:, :], 1e-5).then_inc(made, 1)
            pool.memset(eps6[:, :], 1e-6).then_inc(made, 1)
            pool.iota(iota_e[:, :], pattern=[[1, EXPERTS]], base=0, channel_multiplier=0).then_inc(made, 1)
            pool.iota(iota_p[:, :], pattern=[[0, 1]], base=0, channel_multiplier=1).then_inc(made, 1)
            pool.wait_ge(made, 9)
            pool.affine_select(out=tri[:, :], in_=ones[:, :], compare_op=ALU.is_gt, fill=0.0, base=0,
                               pattern=[[1, P]], channel_multiplier=-1).then_inc(tri_set, 1)
            pool.dma_start(scratch["slots"].rearrange("(p n) o -> p (n o)", p=P), zeros[:, :]).then_inc(zeroed, 16)
            pool.wait_ge(zeroed, 16)

            def step(n, par, at):
                if has(at, 5):
                    t, q = n - 5, 1 - par
                    gate(pool, slot_set, t + (1 + SLOT0), passed)
                    for k in range(2):
                        pool.indirect_dma_start(scratch["slots"], bass.IndirectOffsetOnAxis(ap=slot[:, q, k:k + 1], axis=0),
                                                tok[:, q:q + 1], None).then_inc(scattered, 16)
                    gate(pool, scattered, t * 32 + 32, passed)
                    pool.sem_inc(freed, 1)

            steps(pool, step)

        @block.scalar
        def _(act):
            act.sem_inc(rooted2, ROOTED2_0)
            act.wait_ge(gain_set, 1)
            act.wait_ge(made, 9)

            def step(n, par, at):
                if has(at, 2):
                    t = n - 2
                    act.wait_ge(x2_set, t + (1 + X2_0))
                    act.wait_ge(rooted2, t + ROOTED2_0)
                    nc.scalar.activation(sq2[:, :], x2[:, par, :], ACT.Square, accum_out=ss2[:, :]).then_inc(squared2, 1)
                    act.wait_ge(squared2, t + 1)
                    nc.scalar.activation(rt2[:, :], ss2[:, :], ACT.Sqrt, bias=eps6[:, 0:1], scale=1.0 / D).then_inc(rooted2, 1)
                if has(at, 0):
                    act.wait_ge(o_in[par], uses(n, par) + 16)
                    act.wait_ge(summed, n + SUMMED0)
                    nc.scalar.activation(sq[:, :], o_t[:, par, :], ACT.Square).then_inc(squared, 1)
                    act.wait_ge(summed, n + (1 + SUMMED0))
                    nc.scalar.activation(rth[:, :], ssh[:, :], ACT.Sqrt, bias=eps5[:, 0:1], scale=1.0 / P).then_inc(rooted, 1)
                    act.wait_ge(turned, n + (1 + TURNED0))
                    act.wait_ge(projected, n + (PROJECTED0 - 1))
                    nc.scalar.activation(oT_hi[:, par, :], ps_a[:, :], ACT.Copy, scale=sub_gs[:, 0:1]).then_inc(oT_hi_set, 1)
                if has(at, 2):
                    t = n - 2
                    act.wait_ge(turned2, t + 1)
                    act.wait_ge(routed, t + ROUTED0)
                    nc.scalar.activation(h2T[:, :], ps_c[:, :], ACT.Copy).then_inc(h2T_set, 1)

            steps(act, step)

        @block.vector
        def _(dve):
            dve.sem_inc(summed, SUMMED0)
            dve.sem_inc(oT_lo_set, OT_LO0)
            dve.sem_inc(x2_set, X2_0)
            dve.sem_inc(both_set, BOTH0)
            dve.sem_inc(slot_set, SLOT0)
            dve.sem_inc(freed, FREED0)
            for k in range(2):
                dve.sem_inc(x2_out[k], OUT0)
                dve.sem_inc(h2_out[k], OUT0)
            dve.wait_ge(const_in, 16 * 6)
            nc.vector.tensor_scalar(sub_gs[:, :], sub_g[:, :], 1.0 - LAMBDA_INIT, None, ALU.mult).then_inc(gain_set, 1)
            dve.wait_ge(made, 9)
            nc.vector.tensor_copy(iota_ef[:, :], iota_e[:, :]).then_inc(index_set, 1)
            nc.vector.tensor_copy(iota_pf[:, :], iota_p[:, :]).then_inc(index_set, 1)
            dve.wait_ge(index_set, 2)
            nc.vector.tensor_scalar(tok_f[:, 0:1], iota_pf[:, :], -float(P), None, ALU.add).then_inc(index_set, 1)
            dve.wait_ge(index_set, 3)
            dve.wait_ge(wo_in, 16)
            nc.vector.tensor_copy(wo_hi[:, :, :], wo_raw[:, :, :]).then_inc(wo_hi_set, 1)
            dve.wait_ge(wo_hi_set, 1)
            nc.vector.tensor_tensor(wo_lo[:, :, :], wo_raw[:, :, :], wo_hi[:, :, :].bitcast(F32), ALU.subtract).then_inc(wo_split, 1)

            def chain(done, first):
                k = [0]

                def link(ins, alone=False):
                    k[0] += 1
                    ins.then_inc(done, 1)
                    if alone:
                        gate(dve, done, first + k[0], passed)
                    else:
                        dve.wait_ge(done, first + k[0])
                return link

            def step(n, par, at):
                if has(at, 2):
                    t = n - 2
                    dve.wait_ge(x_in[par], uses(t, par) + 16)
                    dve.wait_ge(projected, t + (1 + PROJECTED0))
                    nc.vector.tensor_tensor(x2[:, par, :], ps_b[:, :], x2[:, par, :], ALU.add).then_inc(x2_set, 1)
                    dve.wait_ge(rooted2, t + (1 + ROOTED2_0))
                    nc.vector.reciprocal(ri2[:, :], rt2[:, :]).then_inc(inverted2, 1)
                    dve.wait_ge(inverted2, t + 1)
                    dve.wait_ge(h2_out[par], uses(t, par) + OUT0)
                    nc.vector.scalar_tensor_tensor(out=h2[:, par, :], in0=x2[:, par, :], scalar=ri2[:, 0:1],
                                                   in1=g2_row[:, :], op0=ALU.mult, op1=ALU.mult).then_inc(h2_set, 1)
                if has(at, 0):
                    dve.wait_ge(squared, n + 1)
                    nc.vector.tensor_reduce(ssh[:, :], sq[:, :].rearrange("p (h e) -> p h e", h=HEADS), AX.X,
                                            ALU.add).then_inc(summed, 1)
                    dve.wait_ge(rooted, n + 1)
                    nc.vector.reciprocal(rih[:, :], rth[:, :]).then_inc(inverted, 1)
                    dve.wait_ge(inverted, n + 1)
                    ot = o_t[:, par, :].rearrange("p (h e) -> p h e", h=HEADS)
                    nc.vector.tensor_tensor(ot, ot, rih[:, :].unsqueeze(2).to_broadcast([P, HEADS, P]),
                                            ALU.mult).then_inc(normed, 1)
                if has(at, 4):
                    choose(n - 4, par)
                if has(at, 5):
                    place(n - 5, 1 - par)
                if has(at, 0):
                    dve.wait_ge(oT_hi_set, n + 1)
                    nc.vector.scalar_tensor_tensor(out=oT_lo[:, par, :], in0=ps_a[:, :], scalar=sub_gs[:, 0:1],
                                                   in1=oT_hi[:, par, :].bitcast(F32), op0=ALU.mult,
                                                   op1=ALU.subtract).then_inc(oT_lo_set, 1)

            def choose(t, q):
                link = chain(chosen, t * 14)
                dve.wait_ge(routed, t + (1 + ROUTED0))
                nc.vector.tensor_tensor(lg[:, 0:GROUPS_E], ps_d[:, 0:GROUPS_E], b_r[:, 0:GROUPS_E], ALU.add)
                link(nc.vector.tensor_tensor(le[:, :], ps_d[:, GROUPS_E:ROUTES], b_r[:, GROUPS_E:], ALU.add), True)
                link(nc.vector.max(gm[:, :], lg[:, :]), True)
                link(nc.vector.max_index(gi[:, :], gm[:, :], lg[:, :]))
                link(nc.vector.tensor_copy(gf[:, :], gi[:, 0:1]))
                nc.vector.tensor_scalar(g8[:, :], gf[:, :], float(PER_GROUP), None, ALU.mult)
                link(nc.vector.tensor_scalar(gmask[:, :], iota_ef[:, 0:GROUPS_E], gf[:, 0:1], None, ALU.is_equal))
                by_group = lambda a: a.rearrange("p (g j) -> p g j", g=GROUPS_E)
                link(nc.vector.tensor_tensor(by_group(em[:, :]), by_group(le[:, :]),
                                             gmask[:, :].unsqueeze(2).to_broadcast([P, GROUPS_E, PER_GROUP]), ALU.mult))
                link(nc.vector.tensor_reduce(es[:, :], em[:, :].rearrange("p (g j) -> p j g", g=GROUPS_E), AX.X, ALU.add), True)
                link(nc.vector.max(ev[:, :], es[:, :]), True)
                link(nc.vector.max_index(ei[:, :], ev[:, :], es[:, :]))
                link(nc.vector.tensor_copy(ef[:, :], ei[:, 0:2]))
                link(nc.vector.tensor_scalar(eid[:, q, :], ef[:, :], g8[:, 0:1], None, ALU.add))
                link(nc.vector.tensor_scalar(own[:, q, 0, :], iota_ef[:, :], eid[:, q, 0:1], None, ALU.is_equal))
                link(nc.vector.tensor_scalar(own[:, q, 1, :], iota_ef[:, :], eid[:, q, 1:2], None, ALU.is_equal))
                nc.vector.tensor_copy(kept[:, bass.ds(t, 1), 0:4].rearrange("p o n -> p (o n)"), lg[:, 0:4])
                nc.vector.tensor_copy(kept[:, bass.ds(t, 1), 4:6].rearrange("p o n -> p (o n)"), ev[:, 0:2])
                link(nc.vector.tensor_copy(e_all[:, bass.ds(t, 1), :].rearrange("p o n -> p (o n)"), eid[:, q, :]))
                nc.vector.tensor_tensor(both[:, q, :], own[:, q, 0, :], own[:, q, 1, :], ALU.add).then_inc(both_set, 1)

            def place(t, q):
                link = chain(placed, t * 6)
                dve.wait_ge(ranked, t + 1)
                for j in range(2):
                    gate(dve, ranked, t + 1, passed)
                    link(nc.vector.tensor_tensor_reduce(junk[:, j, :], own[:, q, j, :], ps_e[:, 0:EXPERTS], 1.0, 0.0,
                                                        ALU.mult, ALU.add, rank[:, q, j:j + 1]))
                nc.vector.tensor_copy(rank_all[:, bass.ds(t, 1), :].rearrange("p o n -> p (o n)"), rank[:, q, :])
                link(nc.vector.scalar_tensor_tensor(out=slot_f[:, :], in0=eid[:, q, :], scalar=float(SEQ),
                                                    in1=rank[:, q, :], op0=ALU.mult, op1=ALU.add))
                link(nc.vector.tensor_scalar(tok_f[:, 0:1], tok_f[:, 0:1], float(P), None, ALU.add))
                dve.wait_ge(freed, t + (FREED0 - 1))
                link(nc.vector.tensor_copy(tok[:, q:q + 1], tok_f[:, 0:1]))
                link(nc.vector.tensor_tensor(before[:, :], before[:, :], both[:, q, :], ALU.add))
                nc.vector.tensor_copy(slot[:, q, :], slot_f[:, :]).then_inc(slot_set, 1)

            steps(dve, step)

            link = chain(tabled, 0)
            dve.wait_ge(counted, 1)
            link(nc.vector.tensor_scalar(cnt_i[:, :], ps_e[:, 0:EXPERTS], float(P - 1), None, ALU.add))
            link(nc.vector.tensor_scalar(nb_i[:, :], cnt_i[:, :], P.bit_length() - 1, None, ALU.logical_shift_right))
            link(nc.vector.tensor_scalar(nb[:, :], nb_i[:, :], 1.0, None, ALU.max))
            link(nc.vector.tensor_tensor_scan(upto[:, :], one_e[:, :], nb[:, :], 0.0, ALU.mult, ALU.add))
            link(nc.vector.tensor_tensor(start[:, :], upto[:, :], nb[:, :], ALU.subtract))
            nc.vector.tensor_copy(tabf[:, 4:5], upto[:, EXPERTS - 1:EXPERTS])
            link(nc.vector.tensor_scalar(cmp[:, :], start[:, :], iota_pf[:, 0:1], None, ALU.is_le))
            link(nc.vector.tensor_reduce(tabf[:, 0:1], cmp[:, :], AX.X, ALU.add))
            link(nc.vector.tensor_tensor(cmp[:, :], cmp[:, :], start[:, :], ALU.mult))
            link(nc.vector.tensor_reduce(tabf[:, 5:6], cmp[:, :], AX.X, ALU.max))
            link(nc.vector.tensor_scalar(cmp[:, :], start[:, :], iota_pf[:, 0:1], None, ALU.is_equal))
            link(nc.vector.tensor_reduce(tabf[:, 3:4], cmp[:, :], AX.X, ALU.max))
            link(nc.vector.tensor_scalar(cmp[:, :], start[:, :], iota_pf[:, 0:1], 1.0, ALU.subtract, ALU.is_equal))
            link(nc.vector.tensor_reduce(tabf[:, 2:3], cmp[:, :], AX.X, ALU.max))
            link(nc.vector.tensor_scalar(tabf[:, 0:1], tabf[:, 0:1], -1.0, None, ALU.add))
            link(nc.vector.tensor_tensor(tabf[:, 6:7], iota_pf[:, 0:1], tabf[:, 5:6], ALU.subtract))
            link(nc.vector.tensor_scalar(tabf[:, 6:7], tabf[:, 6:7], float(P), None, ALU.mult))
            link(nc.vector.scalar_tensor_tensor(out=tabf[:, 1:2], in0=tabf[:, 0:1], scalar=float(SEQ), in1=tabf[:, 6:7],
                                                op0=ALU.mult, op1=ALU.add))
            link(nc.vector.tensor_scalar(tabf[:, 7:8], tabf[:, 4:5], -1.0, float(BLOCKS_MAX), ALU.mult, ALU.add))
            nc.vector.tensor_copy(tabi[:, :], tabf[:, :]).then_inc(tab_set, 1)

        @block.tensor
        def _(pe):
            pe.sem_inc(turned, TURNED0)
            pe.sem_inc(projected, PROJECTED0)
            pe.sem_inc(routed, ROUTED0)
            pe.sem_inc(h2T_set, H2T0)
            pe.wait_ge(tri_set, 1)
            pe.wait_ge(const_in, 16 * 6)
            pe.wait_ge(wo_split, 1)

            def step(n, par, at):
                if has(at, 1):
                    t, q = n - 1, 1 - par
                    pe.wait_ge(oT_lo_set, t + (1 + OT_LO0))
                    pe.wait_ge(x2_set, t + X2_0)
                    k = 0
                    for o, w in ((oT_lo, wo_hi), (oT_hi, wo_lo), (oT_hi, wo_hi)):
                        for c in range(KC):
                            for j in range(2):
                                mm = pe.matmul(ps_b[:, j * 512:(j + 1) * 512], o[:, q, c * P:(c + 1) * P],
                                               w[:, c, j * 512:(j + 1) * 512], start=k == 0, stop=k == 23)
                            k += 1
                    mm.then_inc(projected, 1)
                if has(at, 0):
                    pe.wait_ge(normed, n + 1)
                    pe.wait_ge(oT_lo_set, n + OT_LO0)
                    for c in range(KC):
                        mm = pe.transpose(ps_a[:, c * P:(c + 1) * P], o_t[:, par, c * P:(c + 1) * P], ident[:, :])
                    mm.then_inc(turned, 1)
                if has(at, 2):
                    t = n - 2
                    pe.wait_ge(h2_set, t + 1)
                    pe.wait_ge(h2T_set, t + H2T0)
                    for c in range(KC):
                        mm = pe.transpose(ps_c[:, c * P:(c + 1) * P], h2[:, par, c * P:(c + 1) * P], ident[:, :])
                    mm.then_inc(turned2, 1)
                if has(at, 3):
                    t = n - 3
                    pe.wait_ge(h2T_set, t + (1 + H2T0))
                    pe.wait_ge(both_set, t + BOTH0)
                    for c in range(KC):
                        mm = pe.matmul(ps_d[:, 0:ROUTES], h2T[:, c * P:(c + 1) * P], w_r[:, c, :], start=c == 0,
                                       stop=c == KC - 1)
                    mm.then_inc(routed, 1)
                if has(at, 4):
                    t, q = n - 4, par
                    pe.wait_ge(both_set, t + (1 + BOTH0))
                    pe.wait_ge(slot_set, t + SLOT0)
                    pe.matmul(ps_e[:, 0:EXPERTS], ones[:, :], before[:, :], start=True, stop=False)
                    pe.matmul(ps_e[:, 0:EXPERTS], tri[:, :], both[:, q, :], start=False, stop=True).then_inc(ranked, 1)

            steps(pe, step)
            pe.wait_ge(slot_set, TILES + SLOT0)
            pe.matmul(ps_e[:, 0:EXPERTS], ones[:, :], before[:, :], start=True, stop=True).then_inc(counted, 1)


def run_experts(nc, io, keep, scratch, sem):
    GS, DS = 4, 2
    GC, DC = KC // GS, FC // DS
    with ExitStack() as ctx:
        def sb(name, shape, dt=F32):
            return ctx.enter_context(nc.sbuf_tensor(name, shape, dt))

        gu_raw = sb("gu_raw", [P, GS, GC, 2, FF])
        gu_hi = sb("gu_hi", [P, KC, 2, FF], F32R)
        gu_lo = sb("gu_lo", [P, KC, 2, FF], F32R)
        d_raw = sb("d_raw", [P, DS, DC, D])
        d_hi = sb("d_hi", [P, FC, D], F32R)
        d_lo = sb("d_lo", [P, FC, D], F32R)
        table = sb("block_table", [1, P * 8], I32)
        listed = sb("listed", [P, 1], I32)
        xg = sb("xg", [P, D])
        xT_hi, xT_lo = sb("xT_hi", [P, D], F32R), sb("xT_lo", [P, D], F32R)
        act_g = sb("act_g", [P, FF])
        hid = sb("hid", [P, FF])
        hT_hi, hT_lo = sb("hT_hi", [P, FF], F32R), sb("hT_lo", [P, FF], F32R)
        y_sb = sb("y_sb", [P, D])
        nil = sb("nil", [P, D])
        own = sb("own_all", [P, 2 * TILES, EXPERTS])
        first_row = sb("first_row", [P, 2 * TILES])
        iota_i, iota_f = sb("iota_i4", [P, EXPERTS], I32), sb("iota_f4", [P, EXPERTS])
        dest_f = sb("dest_f", [P, 2 * TILES])
        ps_x = ctx.enter_context(nc.psum_tensor("ps_x", [P, D], F32))
        ps_g = ctx.enter_context(nc.psum_tensor("ps_g", [P, 2, FF], F32))
        ps_h = ctx.enter_context(nc.psum_tensor("ps_h", [P, FF], F32))
        ps_y = ctx.enter_context(nc.psum_tensor("ps_y", [P, D], F32))
        ident, start, e_all, rank_all, dest = (keep[k] for k in ("ident", "start", "e_all", "rank_all", "dest"))
        s = lambda name: sem("d_" + name)
        gu_in, d_in = [s(f"gu_in{j}") for j in range(GS)], [s(f"d_in{j}") for j in range(DS)]
        gu_hi_set, gu_split, gu_ready, gu_used = s("gu_hi"), s("gu_split"), s("gu_ready"), s("gu_used")
        d_hi_set, d_split, d_ready, d_used = s("d_hi"), s("d_split"), s("d_ready"), s("d_used")
        table_in, listed_in, x_in, x_turned = s("table_in"), s("listed_in"), s("x_in"), s("x_turned")
        x_hi_set, x_lo_set, act_set, hid_set = s("x_hi"), s("x_lo"), s("act"), s("hid")
        h_turned, h_hi_set, h_lo_set, y_taken, y_out = s("h_turned"), s("h_hi"), s("h_lo"), s("y_taken"), s("y_out")
        nil_set, nil_out = s("nil_set"), s("nil_out")
        iota_set, found = s("iota"), s("found")
        passed = sem("passed")
        block = ctx.enter_context(nc.Block())
        GU_SPLIT0, D_SPLIT0, D_READY0, D_USED0, X_TURNED0, Y_TAKEN0, Y_OUT0, H_LO0 = GS, DS, DS, DS, 1, 2, 17, 1
        COL_EXPERT, COL_LIST, COL_NEXT, COL_FIRST, COL_BLOCKS, COL_UNUSED = 0, 1, 2, 3, 4, 7

        def look(eng, b, column, least, most):
            return eng.value_load(table[0:1, bass.ds(b * 8 + column, 1)], min_val=least, max_val=most)

        def blocks_of(eng):
            eng.wait_ge(table_in, 16)
            return look(eng, 0, COL_BLOCKS, EXPERTS, BLOCKS_MAX - 1)

        @block.sync
        def _(sp):
            sp.dma_start(table[:, :], scratch["tab"].rearrange("(o p) c -> o (p c)", o=1)).then_inc(table_in, 16)
            with sp.Fori(0, EXPERTS) as e:
                def rows(w, j, n):
                    r = w.rearrange("o e (c p) n -> p (o e) c n", p=P)
                    return r[:, bass.ds(e, 1), j * n:(j + 1) * n, :].rearrange("p o c n -> p (o c) n")

                for j in range(GS):
                    gate(sp, gu_split, e * GS + (j + 1), passed)
                    sp.dma_start(gu_raw[:, j, :, 0, :], rows(io["moe_w_gate"], j, GC)).then_inc(gu_in[j], 16)
                    sp.dma_start(gu_raw[:, j, :, 1, :], rows(io["moe_w_up"], j, GC)).then_inc(gu_in[j], 16)
                for j in range(DS):
                    gate(sp, d_split, e * DS + (j + 1), passed)
                    sp.dma_start(d_raw[:, j, :, :], rows(io["moe_w_down"], j, DC)).then_inc(d_in[j], 16)
            n = blocks_of(sp)
            unused = look(sp, 0, COL_UNUSED, 1, BLOCKS_MAX - EXPERTS)
            sp.wait_ge(nil_set, 1)
            with sp.Fori(n, BLOCKS_MAX) as z:
                sp.dma_start(scratch["y"].rearrange("(b p) d -> b p d", p=P)[bass.ds(z, 1)].rearrange("o p d -> (o p) d"),
                             nil[:, :]).then_inc(nil_out, 16)
            gate(sp, nil_out, unused * 16, passed)

        @block.gpsimd
        def _(pool):
            pool.memset(nil[:, :], 0.0).then_inc(nil_set, 1)
            pool.iota(iota_i[:, :], pattern=[[1, EXPERTS]], base=0, channel_multiplier=0).then_inc(iota_set, 1)
            n = blocks_of(pool)
            with pool.Fori(0, n + 1) as b:
                at = look(pool, b, COL_LIST, 0, SLOTS - P)
                gate(pool, x_turned, b + X_TURNED0, passed)
                pool.dma_start(listed[:, :], scratch["slots"][bass.ds(at, P), :]).then_inc(listed_in, 16)
                gate(pool, listed_in, b * 16 + 16, passed)
                pool.indirect_dma_start(xg[:, :], None, scratch["h2"],
                                        bass.IndirectOffsetOnAxis(ap=listed[:, 0:1], axis=0)).then_inc(x_in, 16)

        @block.scalar
        def _(act):
            n = blocks_of(act)

            def gu_high(e, freed):
                for j in range(GS):
                    if freed is not None:
                        act.wait_ge(gu_used, freed + (j + 1))
                    act.wait_ge(gu_in[j], e * 32 + 32)
                    nc.scalar.activation(gu_hi[:, j * GC:(j + 1) * GC], gu_raw[:, j], ACT.Copy).then_inc(gu_hi_set, 1)

            def d_high(e, freed):
                for j in range(DS):
                    if freed is not None:
                        act.wait_ge(d_used, freed + (j + 1))
                    act.wait_ge(d_in[j], e * 16 + 16)
                    nc.scalar.activation(d_hi[:, j * DC:(j + 1) * DC, :], d_raw[:, j], ACT.Copy).then_inc(d_hi_set, 1)

            def x_high(b):
                act.wait_ge(x_turned, b + (1 + X_TURNED0))
                nc.scalar.activation(xT_hi[:, :], ps_x[:, :], ACT.Copy).then_inc(x_hi_set, 1)

            def take_y(k):
                act.wait_ge(d_used, k * DS + D_USED0)
                act.wait_ge(y_out, k * 16 + (Y_OUT0 - 16))
                nc.scalar.activation(y_sb[:, :], ps_y[:, :], ACT.Copy).then_inc(y_taken, 1)

            def store_y(k):
                gate(act, y_taken, k + Y_TAKEN0, passed)
                act.dma_start(scratch["y"].rearrange("(b p) d -> b p d", p=P)[bass.ds(k - 1, 1)].rearrange("o p d -> (o p) d"),
                              y_sb[:, :]).then_inc(y_out, 16)

            def iteration(b, first):
                e = look(act, b, COL_EXPERT, 0, EXPERTS - 1)
                more = look(act, b, COL_NEXT, 0, 1)
                new = look(act, b, COL_FIRST, 0, 1)
                with act.If(more > 0):
                    gu_high(e + 1, b * GS)
                act.wait_ge(gu_used, b * GS + GS)
                nc.scalar.activation(act_g[:, :], ps_g[:, 0, :], ACT.Silu).then_inc(act_set, 1)
                x_high(b + 1)
                if not first:
                    take_y(b)
                    with act.If(new > 0):
                        d_high(e, b * DS + (D_USED0 - DS))
                act.wait_ge(h_turned, b + 1)
                nc.scalar.activation(hT_hi[:, :], ps_h[:, :], ACT.Copy).then_inc(h_hi_set, 1)
                if not first:
                    store_y(b)

            gu_high(0, None)
            d_high(0, None)
            x_high(0)
            iteration(0, True)
            with act.Fori(1, n) as b:
                iteration(b, False)
            take_y(n)
            store_y(n)
            act.wait_ge(y_out, n * 16 + Y_OUT0)
            act.sem_inc(passed, 1)

        @block.vector
        def _(dve):
            dve.sem_inc(gu_split, GU_SPLIT0)
            dve.sem_inc(d_split, D_SPLIT0)
            dve.sem_inc(d_ready, D_READY0)
            dve.sem_inc(h_lo_set, H_LO0)
            n = blocks_of(dve)

            def gu_low(e):
                for j in range(GS):
                    dve.wait_ge(gu_hi_set, e * GS + (j + 1))
                    nc.vector.tensor_tensor(gu_lo[:, j * GC:(j + 1) * GC], gu_raw[:, j],
                                            gu_hi[:, j * GC:(j + 1) * GC].bitcast(F32), ALU.subtract).then_inc(gu_split, 1)
                    dve.wait_ge(gu_split, e * GS + (j + 1 + GU_SPLIT0))
                    dve.sem_inc(gu_ready, 1)

            def d_low(e):
                for j in range(DS):
                    dve.wait_ge(d_hi_set, e * DS + (j + 1))
                    nc.vector.tensor_tensor(d_lo[:, j * DC:(j + 1) * DC, :], d_raw[:, j],
                                            d_hi[:, j * DC:(j + 1) * DC, :].bitcast(F32), ALU.subtract).then_inc(d_split, 1)
                    dve.wait_ge(d_split, e * DS + (j + 1 + D_SPLIT0))
                    dve.sem_inc(d_ready, 1)

            def x_low(b):
                dve.wait_ge(x_hi_set, b + 1)
                nc.vector.tensor_tensor(xT_lo[:, :], ps_x[:, :], xT_hi[:, :].bitcast(F32), ALU.subtract).then_inc(x_lo_set, 1)

            def iteration(b, first):
                e = look(dve, b, COL_EXPERT, 0, EXPERTS - 1)
                more = look(dve, b, COL_NEXT, 0, 1)
                new = look(dve, b, COL_FIRST, 0, 1)
                with dve.If(more > 0):
                    gu_low(e + 1)
                with dve.Else():
                    dve.sem_inc(gu_ready, GS)
                dve.wait_ge(act_set, b + 1)
                nc.vector.tensor_tensor(hid[:, :], act_g[:, :], ps_g[:, 1, :], ALU.mult).then_inc(hid_set, 1)
                x_low(b + 1)
                if not first:
                    with dve.If(new > 0):
                        d_low(e)
                    with dve.Else():
                        dve.sem_inc(d_ready, DS)
                dve.wait_ge(h_hi_set, b + 1)
                nc.vector.tensor_tensor(hT_lo[:, :], ps_h[:, :], hT_hi[:, :].bitcast(F32), ALU.subtract).then_inc(h_lo_set, 1)

            gu_low(0)
            d_low(0)
            x_low(0)
            iteration(0, True)
            with dve.Fori(1, n) as b:
                iteration(b, False)

            k = [0]

            def link(ins):
                k[0] += 1
                ins.then_inc(found, 1)
                dve.wait_ge(found, k[0])

            pairs = 2 * TILES
            dve.wait_ge(iota_set, 1)
            link(nc.vector.tensor_copy(iota_f[:, :], iota_i[:, :]))
            link(nc.vector.tensor_tensor(own[:, :, :], iota_f[:, :].unsqueeze(1).to_broadcast([P, pairs, EXPERTS]),
                                         e_all[:, :, :].rearrange("p t k -> p (t k)").unsqueeze(2)
                                         .to_broadcast([P, pairs, EXPERTS]), ALU.is_equal))
            link(nc.vector.tensor_tensor(own[:, :, :], own[:, :, :],
                                         start[:, :].unsqueeze(1).to_broadcast([P, pairs, EXPERTS]), ALU.mult))
            link(nc.vector.tensor_reduce(first_row[:, :], own[:, :, :], AX.X, ALU.add))
            link(nc.vector.scalar_tensor_tensor(out=dest_f[:, :], in0=first_row[:, :], scalar=float(P),
                                                in1=rank_all[:, :, :].rearrange("p t k -> p (t k)"),
                                                op0=ALU.mult, op1=ALU.add))
            link(nc.vector.tensor_copy(dest[:, :], dest_f[:, :]))

        @block.tensor
        def _(pe):
            pe.sem_inc(x_turned, X_TURNED0)
            pe.sem_inc(y_taken, Y_TAKEN0)
            pe.sem_inc(y_out, Y_OUT0)
            pe.sem_inc(d_used, D_USED0)
            n = blocks_of(pe)

            def turn_x(b):
                pe.wait_ge(x_in, b * 16 + 16)
                for c in range(KC):
                    mm = pe.transpose(ps_x[:, c * P:(c + 1) * P], xg[:, c * P:(c + 1) * P], ident[:, :])
                mm.then_inc(x_turned, 1)

            def gate_up(b):
                pe.wait_ge(x_lo_set, b + 1)
                for c in range(KC):
                    if c % GC == 0:
                        pe.wait_ge(gu_ready, b * GS + (c // GC + 1))
                    cs = slice(c * P, (c + 1) * P)
                    for k, (x, w) in enumerate(((xT_lo, gu_hi), (xT_hi, gu_lo), (xT_hi, gu_hi))):
                        for half in range(2):
                            mm = pe.matmul(ps_g[:, half, :], x[:, cs], w[:, c, half, :], start=c == 0 and k == 0,
                                           stop=c == KC - 1 and k == 2)
                    if c % GC == GC - 1:
                        mm.then_inc(gu_used, 1)

            def turn_h(b):
                pe.wait_ge(hid_set, b + 1)
                for f in range(FC):
                    mm = pe.transpose(ps_h[:, f * P:(f + 1) * P], hid[:, f * P:(f + 1) * P], ident[:, :])
                mm.then_inc(h_turned, 1)

            def down(k):
                pe.wait_ge(h_lo_set, k + H_LO0)
                pe.wait_ge(y_taken, k + (Y_TAKEN0 - 1))
                for f in range(FC):
                    if f % DC == 0:
                        pe.wait_ge(d_ready, k * DS + (f // DC + 1 + D_READY0 - DS))
                    fs = slice(f * P, (f + 1) * P)
                    for term, (h, w) in enumerate(((hT_lo, d_hi), (hT_hi, d_lo), (hT_hi, d_hi))):
                        for half in range(2):
                            hs = slice(half * 512, (half + 1) * 512)
                            mm = pe.matmul(ps_y[:, hs], h[:, fs], w[:, f, hs], start=f == 0 and term == 0,
                                           stop=f == FC - 1 and term == 2)
                    if f % DC == DC - 1:
                        mm.then_inc(d_used, 1)

            turn_x(0)
            gate_up(0)
            turn_x(1)
            turn_h(0)
            with pe.Fori(1, n) as b:
                gate_up(b)
                turn_x(b + 1)
                down(b)
                turn_h(b)
            down(n)


def finish(nc, io, keep, scratch, sem, out):
    RING = 4
    with ExitStack() as ctx:
        def sb(name, shape, dt=F32):
            return ctx.enter_context(nc.sbuf_tensor(name, shape, dt))

        y = sb("y_two", [P, RING, 2, D])
        acc = sb("acc", [P, RING, D])
        sq = sb("sq5", [P, D])
        g_row = sb("g5_row", [P, D])
        rows = sb("rows", [P, RING, 2], I32)
        peak = sb("peak5", [P, TILES])
        e_l = sb("e_l", [P, TILES, GROUPS_E])
        e_sum, e_v = sb("e_sum", [P, TILES]), sb("e_v", [P, TILES])
        den = sb("den", [P, TILES])
        w_all = sb("w_all", [P, 2, TILES])
        eps = sb("eps55", [P, 1])
        ss, rt, ri = sb("ss5", [P, RING]), sb("rt5", [P, RING]), sb("ri5", [P, RING])
        kept, dest = keep["kept"], keep["dest"]
        s = lambda name: sem("e_" + name)
        g_in, x_in, y_in = s("g_in"), [s(f"x_in{i}") for i in range(RING)], [s(f"y_in{i}") for i in range(RING)]
        rows_set, weigh, exped, mixed, eps_set = s("rows"), s("weigh"), s("exped"), s("mixed"), s("eps")
        added, squared, rooted, inverted, done = s("added"), s("squared"), s("rooted"), s("inverted"), s("done")
        stored = [s(f"stored{i}") for i in range(RING)]
        passed = sem("passed")
        block = ctx.enter_context(nc.Block())
        ADDED0, STORED0, SQUARED0 = RING, 1, 1
        out_rows = out.rearrange("o (t p) d -> (o t) p d", p=P)

        @block.sync
        def _(sp):
            sp.dma_start(g_row[:, :], io["norm_final"].rearrange("(o d) -> o d", o=1).to_broadcast([P, D])).then_inc(g_in, 16)

            def load(t, i):
                gate(sp, stored[i], t * 4 - 4 * i + STORED0 if i else t * 4 + STORED0, passed)
                sp.dma_start(acc[:, i, :], scratch["x2"].rearrange("(t p) d -> t p d", p=P)[bass.ds(t, 1)]
                             .rearrange("o p d -> (o p) d")).then_inc(x_in[i], 16)

            for i in range(RING):
                load(i, i)

            def store(t, i):
                gate(sp, done, t + 1, passed)
                sp.dma_start(out_rows[bass.ds(t, 1)].rearrange("o p d -> (o p) d"), acc[:, i, :]).then_inc(stored[i], 16)

            with sp.Fori(0, TILES // RING - 1) as q:
                for i in range(RING):
                    store(q * RING + i, i)
                    if i >= 1:
                        load(q * RING + (RING + i - 1), i - 1)
                load(q * RING + (2 * RING - 1), RING - 1)
            for i in range(RING):
                store(TILES - RING + i, i)
            for i in range(RING):
                sp.wait_ge(stored[i], 16 * TILES // RING + STORED0)

        @block.gpsimd
        def _(pool):
            pool.memset(eps[:, :], 1e-6).then_inc(eps_set, 1)
            with pool.Fori(0, TILES // RING) as q:
                for i in range(RING):
                    gate(pool, added, q * RING + (i + 1), passed)
                    pool.tensor_copy(rows[:, i, :], dest[:, bass.ds(q * (2 * RING) + 2 * i, 2)]).then_inc(rows_set, 1)
                    gate(pool, rows_set, q * RING + (i + 1), passed)
                    for k in range(2):
                        pool.indirect_dma_start(y[:, i, k, :], None, scratch["y"],
                                                bass.IndirectOffsetOnAxis(ap=rows[:, i, k:k + 1], axis=0)).then_inc(y_in[i], 16)

        @block.scalar
        def _(act):
            act.sem_inc(squared, SQUARED0)
            act.wait_ge(weigh, 3)
            nc.scalar.activation(e_l[:, :, :], e_l[:, :, :], ACT.Exp).then_inc(exped, 1)
            nc.scalar.activation(e_v[:, :], e_v[:, :], ACT.Exp).then_inc(exped, 1)
            act.wait_ge(eps_set, 1)
            with act.Fori(0, TILES // RING) as q:
                for i in range(RING):
                    act.wait_ge(added, q * RING + (i + 1 + ADDED0))
                    act.wait_ge(squared, q * RING + (i + SQUARED0))
                    nc.scalar.activation(sq[:, :], acc[:, i, :], ACT.Square, accum_out=ss[:, i:i + 1]).then_inc(squared, 1)
                    act.wait_ge(squared, q * RING + (i + 1 + SQUARED0))
                    nc.scalar.activation(rt[:, i:i + 1], ss[:, i:i + 1], ACT.Sqrt, bias=eps[:, 0:1],
                                         scale=1.0 / D).then_inc(rooted, 1)

        @block.vector
        def _(dve):
            for i in range(RING):
                dve.sem_inc(stored[i], STORED0)
            dve.sem_inc(added, ADDED0)
            k = [0]

            def link(ins):
                k[0] += 1
                ins.then_inc(weigh, 1)
                dve.wait_ge(weigh, k[0])

            link(nc.vector.tensor_reduce(peak[:, :], kept[:, :, 0:GROUPS_E], AX.X, ALU.max))
            link(nc.vector.tensor_tensor(e_l[:, :, :], kept[:, :, 0:GROUPS_E],
                                         peak[:, :].unsqueeze(2).to_broadcast([P, TILES, GROUPS_E]), ALU.subtract))
            link(nc.vector.tensor_tensor(e_v[:, :], kept[:, :, 5], kept[:, :, 4], ALU.subtract))
            dve.wait_ge(exped, 2)
            link(nc.vector.tensor_reduce(e_sum[:, :], e_l[:, :, :], AX.X, ALU.add))
            link(nc.vector.scalar_tensor_tensor(out=den[:, :], in0=e_v[:, :], scalar=1.0, in1=e_sum[:, :],
                                                op0=ALU.add, op1=ALU.mult))
            link(nc.vector.reciprocal(w_all[:, 0, :], den[:, :]))
            link(nc.vector.tensor_tensor(w_all[:, 1, :], w_all[:, 0, :], e_v[:, :], ALU.mult))
            dve.wait_ge(g_in, 16)

            def scale(q, i):
                dve.wait_ge(rooted, q * RING + (i + 1))
                nc.vector.reciprocal(ri[:, i:i + 1], rt[:, i:i + 1]).then_inc(inverted, 1)
                dve.wait_ge(inverted, q * RING + (i + 1))
                nc.vector.scalar_tensor_tensor(out=acc[:, i, :], in0=acc[:, i, :], scalar=ri[:, i:i + 1], in1=g_row[:, :],
                                               op0=ALU.mult, op1=ALU.mult).then_inc(done, 1)

            with dve.Fori(0, TILES // RING) as q:
                for i in range(RING):
                    dve.wait_ge(x_in[i], q * 16 + 16)
                    dve.wait_ge(y_in[i], q * 32 + 32)
                    a = acc[:, i, :]
                    nc.vector.scalar_tensor_tensor(out=a, in0=y[:, i, 0, :], scalar=w_all[:, 0, bass.ds(q * RING + i, 1)],
                                                   in1=a, op0=ALU.mult, op1=ALU.add).then_inc(mixed, 1)
                    dve.wait_ge(mixed, q * RING + (i + 1))
                    nc.vector.scalar_tensor_tensor(out=a, in0=y[:, i, 1, :], scalar=w_all[:, 1, bass.ds(q * RING + i, 1)],
                                                   in1=a, op0=ALU.mult, op1=ALU.add).then_inc(added, 1)
                    if i >= 1:
                        scale(q, i - 1)
                scale(q, RING - 1)


def build(nc, io, out, stages=4):
    with ExitStack() as ctx:
        sems = {}

        def sem(name):
            if name not in sems:
                sems[name] = ctx.enter_context(nc.semaphore(name))
            return sems[name]

        def sb(name, shape, dt=F32):
            return ctx.enter_context(nc.sbuf_tensor(name, shape, dt))

        keep = {"ident": sb("ident", [P, P]), "ident_set": sem("ident_set"), "start": sb("start", [P, 32]),
                "kept": sb("kept", [P, TILES, 6]), "e_all": sb("e_all", [P, TILES, 2]),
                "rank_all": sb("rank_all", [P, TILES, 2]), "dest": sb("dest", [P, 2 * TILES], I32)}
        scratch = {
            "qk": nc.dram_tensor("qk", (2 * HEADS, 2, P, SEQ), F32).ap(),
            "v": nc.dram_tensor("v", (HEADS, TILES, P, 2 * P), F32).ap(),
            "z": nc.dram_tensor("z_rows", (HEADS, 3 * P), F32).ap(),
            "near": nc.dram_tensor("near_rows", (HEADS, P, 2 * P), F32).ap(),
            "o": nc.dram_tensor("o_rows", (SEQ, D), F32).ap(),
            "x2": nc.dram_tensor("x2_rows", (SEQ, D), F32).ap(),
            "h2": nc.dram_tensor("h2_rows", (SEQ, D), F32).ap(),
            "slots": nc.dram_tensor("slots", (SLOTS, 1), I32).ap(),
            "y": nc.dram_tensor("y_rows", (BLOCKS_MAX * P, D), F32).ap(),
            "tab": nc.dram_tensor("tab", (P, 8), I32).ap(),
        }
        project(nc, io, keep, scratch, sem)
        attend(nc, io, keep, scratch, sem)
        if stages == 2:
            with nc.Block() as block:
                @block.sync
                def _(sp):
                    sp.dma_start(out[0], scratch["o"]).then_inc(sem("z"), 16)
                    sp.wait_ge(sem("z"), 16)
            return
        mix_and_route(nc, io, keep, scratch, sem)
        if stages == 3:
            with nc.Block() as block:
                @block.sync
                def _(sp):
                    z = sem("z")
                    sp.dma_start(out[0], scratch["x2"]).then_inc(z, 16)
                    sp.dma_start(out[1], scratch["h2"]).then_inc(z, 16)
                    sp.dma_start(out[2], keep["e_all"][:, :, :]).then_inc(z, 16)
                    sp.dma_start(out[3], keep["rank_all"][:, :, :]).then_inc(z, 16)
                    sp.dma_start(out[4], scratch["tab"].bitcast(F32)).then_inc(z, 16)
                    sp.wait_ge(z, 80)
            return
        run_experts(nc, io, keep, scratch, sem)
        finish(nc, io, keep, scratch, sem, out[0])


_INS = ["x", "rel_bias_table", "norm_mix", "norm_ffn", "norm_final", "diff_w_in", "diff_lambda_qk", "diff_subln",
        "diff_w_out", "moe_w_group", "moe_b_group", "moe_w_expert", "moe_b_expert", "moe_w_gate", "moe_w_up",
        "moe_w_down"]


def distance_buckets(buckets=32, most=128):
    import math
    import numpy as np

    distance = np.maximum(2 * P - 1 - np.arange(3 * P), 0)
    exact = buckets // 2
    f = np.maximum(distance, exact).astype(np.float32)
    far = exact + (np.log(f / exact) / math.log(most / exact) * (buckets - exact)).astype(np.int32)
    bucket = np.where(distance < exact, distance, np.minimum(far, buckets - 1))
    return (np.arange(buckets)[:, None] == bucket[None, :]).astype(np.float32)


def kernel(**inputs):
    import numpy as np
    import concourse.bacc as bacc
    from concourse.bass_utils import run_bass_kernel_spmd as run

    nc = bacc.Bacc("TRN2", target_bir_lowering=False, num_devices=1)
    arrays, io = {}, {}
    for name in _INS:
        a = np.ascontiguousarray(inputs[name])
        arrays["in_" + name] = a
        io[name] = nc.dram_tensor("in_" + name, a.shape, mybir.dt.from_np(a.dtype), kind="ExternalInput").ap()
    a = distance_buckets()
    arrays["in_bucket_of_distance"] = a
    io["bucket_of_distance"] = nc.dram_tensor("in_bucket_of_distance", a.shape, F32, kind="ExternalInput").ap()
    OUT = [(1, SEQ, D)]
    outs = [nc.dram_tensor("out_%d" % i, s, F32, kind="ExternalOutput").ap() for i, s in enumerate(OUT)]
    build(nc, io, outs, 4)
    r = run(nc, [arrays], core_ids=[0])
    got = tuple(r.results[0]["out_%d" % i] for i in range(len(OUT)))
    return got if len(got) > 1 else got[0]
```

```python
from contextlib import ExitStack

import concourse.bass as bass
from concourse import mybir

F32 = mybir.dt.float32
F32R = mybir.dt.float32r
I32 = mybir.dt.int32
U32 = mybir.dt.uint32
ALU = mybir.AluOpType
ACT = mybir.ActivationFunctionType
AX = mybir.AxisListType

P = 128
SEQ = 2048
D = 1024
TILES = SEQ // P
KC = D // P
HEADS = 8
HALF = 64
NEG = -1e30
LOWEST = -3e38
LAMBDA_INIT = 0.8 - 0.6
POOL_NOT = 20


def gate(eng, sem, value, passed):
    eng.wait_ge(sem, value)
    eng.sem_inc(passed, 1)


def project(nc, io, keep, scratch, sem):
    GROUPS = SEQ // 512
    WB = 256
    QKB = 2 * D // WB
    VB = D // WB
    BLOCKS = QKB + VB
    x_rows = io["x"].rearrange("o (t p) d -> (o t) p d", p=P)
    w_rows = io["diff_w_in"].rearrange("o (c p) n -> p (o c) n", p=P)
    with ExitStack() as ctx:
        def sb(name, shape, dt=F32):
            return ctx.enter_context(nc.sbuf_tensor(name, shape, dt))

        hnT_hi = sb("hnT_hi", [P, KC, SEQ], F32R)
        hnT_lo = sb("hnT_lo", [P, KC, SEQ], F32R)
        w_raw = sb("w_raw", [P, KC, WB])
        w_hi = sb("w_hi", [P, 2, KC, WB], F32R)
        w_lo = sb("w_lo", [P, 2, KC, WB], F32R)
        stage = sb("stage", [P, 4, 2 * 512], F32R)
        g_row = sb("g_row", [P, D])
        xt = sb("xt", [P, 4, D])
        sumsq = sb("sumsq", [P, 2, 4])
        root = sb("root", [P, 2, 4])
        rstd = sb("rstd", [P, 2, 4])
        eps = sb("eps", [P, 1])
        ps = ctx.enter_context(nc.psum_tensor("ps1", [P, 8, 512], F32))
        ident = keep["ident"]
        s = lambda name: sem("a_" + name)
        x_in = [s(f"x_in{i}") for i in range(4)]
        g_in, eps_set, w_in, w_split = s("g_in"), s("eps_set"), s("w_in"), s("w_split")
        squared, rooted, inverted, normed = s("squared"), s("rooted"), s("inverted"), s("normed")
        turned, hn_hi, hn_lo = s("turned"), s("hn_hi"), s("hn_lo")
        filled, out_hi, out_lo, w_hi_set = s("filled"), s("out_hi"), s("out_lo"), s("w_hi_set")
        stored = [s(f"stored{i}") for i in range(4)]
        passed = sem("passed")
        ident_set = keep["ident_set"]
        block = ctx.enter_context(nc.Block())
        BANKS = 8
        MEASURED = 6
        TURNED0, HN_LO0, NORMED0, INVERTED0, SQUARED0 = 4, 2, 1, 1, 1
        QK_FILLS = QKB * BANKS
        V_FILLS = VB * TILES

        def x_tile(g, i):
            return (xt if g % 2 == 0 else stage.bitcast(F32))[:, i, :]

        def turned_tile(t):
            return ps[:, (t % 3) * 2:(t % 3) * 2 + 2, :].rearrange("p a (b t) -> p (a b) t", t=P)

        @block.sync
        def _(sp):
            sp.dma_start(g_row[:, :], io["norm_mix"].to_broadcast([P, D])).then_inc(g_in, 16)
            for g in range(GROUPS):
                for i in range(4):
                    if g >= 2:
                        sp.wait_ge(turned, (g - 2) * 4 + i + 1 + TURNED0)
                    sp.dma_start(x_tile(g, i), x_rows[g * 4 + i]).then_inc(x_in[g % 2 * 2 + i // 2], 16)
            with sp.Fori(0, QKB) as b:
                for n in range(8):
                    sp.wait_ge(out_lo, b * 8 + (BANKS + n + 1))
                    dst = scratch["qk"][bass.ds(b * 2 + n // 4, 1)].rearrange("o h p t -> p (o h) t")
                    sp.dma_start(dst[:, :, (n % 4) * 512:(n % 4) * 512 + 512],
                                 stage[:, n % 4, :].bitcast(F32).rearrange("p (h t) -> p h t", h=2)).then_inc(stored[n % 4], 16)
            with sp.Fori(0, VB) as b:
                for n in range(TILES):
                    sp.wait_ge(out_lo, b * TILES + (BANKS + QK_FILLS + n + 1))
                    dst = scratch["v"][bass.ds(b * 2, 2), n].rearrange("h p e -> p h e")
                    sp.dma_start(dst, stage[:, n % 4, 0:512].bitcast(F32).rearrange("p (h e) -> p h e", h=2)
                                 ).then_inc(stored[n % 4], 16)
            for i in range(4):
                sp.wait_ge(stored[i], 16 * (QK_FILLS + V_FILLS) // 4 + 1)

        @block.gpsimd
        def _(pool):
            pool.memset(ident[:, :], 1.0).then_inc(ident_set, 1)
            pool.wait_ge(ident_set, 1)
            pool.affine_select(out=ident[:, :], in_=ident[:, :], compare_op=ALU.is_equal, fill=0.0, base=0,
                               pattern=[[-1, P]], channel_multiplier=1).then_inc(ident_set, 1)
            pool.memset(eps[:, :], 1e-6).then_inc(eps_set, 1)
            with pool.Fori(0, BLOCKS) as b:
                gate(pool, w_split, b + 1, passed)
                pool.dma_start(w_raw[:, :, :], w_rows[:, :, bass.ds(b * WB, WB)]).then_inc(w_in, 16)

        @block.scalar
        def _(act):
            act.sem_inc(squared, 1)
            act.wait_ge(eps_set, 1)

            def measure(t):
                g, i = t // 4, t % 4
                act.wait_ge(x_in[g % 2 * 2 + i // 2], g // 2 * 32 + 32)
                act.wait_ge(squared, t + SQUARED0)
                nc.scalar.activation(ps[:, 6:8, :].rearrange("p a b -> p (a b)"), x_tile(g, i), ACT.Square,
                                     accum_out=sumsq[:, g % 2, i:i + 1]).then_inc(squared, 1)
                if i == 3:
                    act.wait_ge(squared, t + 1 + SQUARED0)
                    if g >= 2:
                        act.wait_ge(inverted, g - 1 + INVERTED0)
                    nc.scalar.activation(root[:, g % 2, :], sumsq[:, g % 2, :], ACT.Sqrt, bias=eps[:, 0:1],
                                         scale=1.0 / D).then_inc(rooted, 1)

            for t in range(MEASURED):
                measure(t)
            for t in range(TILES):
                act.wait_ge(turned, t + 1 + TURNED0)
                nc.scalar.activation(hnT_hi[:, :, t * P:(t + 1) * P], turned_tile(t), ACT.Copy).then_inc(hn_hi, 1)
                if t + MEASURED < TILES:
                    measure(t + MEASURED)

            def take(fill, n, slot_uses, dst, src):
                act.wait_ge(filled, fill + 1)
                act.wait_ge(stored[n % 4], slot_uses + 1)
                nc.scalar.activation(dst, src, ACT.Copy).then_inc(out_hi, 1)

            with act.Fori(0, QKB) as b:
                for n in range(8):
                    take(b * 8 + n + 1, n, b * 32 + 16 * (n // 4), stage[:, n % 4, 0:512], ps[:, n, :])
            with act.Fori(0, VB) as b:
                for n in range(TILES):
                    take(b * TILES + (QK_FILLS + n + 1), n, b * 64 + (QKB * 32 + 16 * (n // 4)),
                         stage[:, n % 4, 0:512].rearrange("p (h e) -> p h e", h=2)[:, :, 0:P],
                         ps[:, n % 8, 0:WB].rearrange("p (h e) -> p h e", h=2))

        @block.vector
        def _(dve):
            dve.sem_inc(out_lo, BANKS)
            dve.sem_inc(hn_lo, 2)
            for one in [w_split, inverted, normed, *stored]:
                dve.sem_inc(one, 1)
            dve.wait_ge(g_in, 16)

            def scale(t):
                g, i = t // 4, t % 4
                if i == 0:
                    dve.wait_ge(rooted, g + 1)
                    if g >= 2:
                        dve.wait_ge(normed, (g - 1) * 4 + NORMED0)
                    nc.vector.reciprocal(rstd[:, g % 2, :], root[:, g % 2, :]).then_inc(inverted, 1)
                    dve.wait_ge(inverted, g + 1 + INVERTED0)
                nc.vector.scalar_tensor_tensor(out=x_tile(g, i), in0=x_tile(g, i), scalar=rstd[:, g % 2, i:i + 1],
                                               in1=g_row[:, :], op0=ALU.mult, op1=ALU.mult).then_inc(normed, 1)

            def split(b, slot, freed=None):
                dve.wait_ge(w_in, b * 16 + 16)
                if freed is not None:
                    dve.wait_ge(filled, freed + 1)
                nc.vector.tensor_copy(w_hi[:, slot], w_raw[:, :, :]).then_inc(w_hi_set, 1)
                dve.wait_ge(w_hi_set, b + 1)
                nc.vector.tensor_tensor(w_lo[:, slot], w_raw[:, :, :], w_hi[:, slot].bitcast(F32),
                                        ALU.subtract).then_inc(w_split, 1)

            def take(fill, dst, hi, src):
                dve.wait_ge(out_hi, fill)
                nc.vector.tensor_tensor(dst, src, hi.bitcast(F32), ALU.subtract).then_inc(out_lo, 1)

            split(0, 0)
            scale(0)
            scale(1)
            for t in range(TILES):
                dve.wait_ge(hn_hi, t + 1)
                nc.vector.tensor_tensor(hnT_lo[:, :, t * P:(t + 1) * P], turned_tile(t),
                                        hnT_hi[:, :, t * P:(t + 1) * P].bitcast(F32), ALU.subtract).then_inc(hn_lo, 1)
                if t + 2 < TILES:
                    scale(t + 2)
            with dve.Fori(0, QKB // 2) as b2:
                for half in range(2):
                    split(b2 * 2 + half + 1, 1 - half, b2 * 16 + half * 8)
                    for n in range(8):
                        take(b2 * 16 + half * 8 + n + 1, stage[:, n % 4, 512:1024], stage[:, n % 4, 0:512], ps[:, n, :])
            for b in range(VB):
                if b + 1 < VB:
                    split(QKB + b + 1, (b + 1) % 2, QK_FILLS + b * TILES)
                for n in range(TILES):
                    out = stage[:, n % 4, 0:512].rearrange("p (h e) -> p h e", h=2)
                    take(QK_FILLS + b * TILES + n + 1, out[:, :, P:2 * P], out[:, :, 0:P],
                         ps[:, n % 8, 0:WB].rearrange("p (h e) -> p h e", h=2))

        @block.tensor
        def _(pe):
            pe.wait_ge(ident_set, 2)
            pe.sem_inc(turned, 4)
            pe.sem_inc(filled, 1)
            for t in range(TILES):
                pe.wait_ge(normed, t + 1 + NORMED0)
                if t >= 3:
                    pe.wait_ge(hn_lo, t - 2 + HN_LO0)
                for c in range(KC):
                    mm = pe.transpose(ps[:, (t % 3) * 2 + c // 4, (c % 4) * P:(c % 4 + 1) * P],
                                      x_tile(t // 4, t % 4)[:, c * P:(c + 1) * P], ident[:, :])
                mm.then_inc(turned, 1)

            TERMS = ((w_lo, hnT_hi), (w_hi, hnT_lo), (w_hi, hnT_hi))
            pe.wait_ge(hn_lo, TILES + 2)
            with pe.Fori(0, QKB // 2) as b2:
                for half in range(2):
                    pe.wait_ge(w_split, b2 * 2 + (half + 2))
                    for n in range(8):
                        pe.wait_ge(out_lo, b2 * 16 + (half * 8 + n + 1))
                        k = 0
                        for w, h in TERMS:
                            for c in range(KC):
                                mm = pe.matmul(ps[:, n, :], w[:, half, c, (n // 4) * P:(n // 4 + 1) * P],
                                               h[:, c, (n % 4) * 512:(n % 4 + 1) * 512], start=k == 0, stop=k == 23)
                                k += 1
                        mm.then_inc(filled, 1)
            with pe.Fori(0, VB // 2) as b2:
                for half in range(2):
                    pe.wait_ge(w_split, b2 * 2 + (QKB + half + 2))
                    for n in range(TILES):
                        pe.wait_ge(out_lo, b2 * (2 * TILES) + (QK_FILLS + half * TILES + n + 1))
                        k = 0
                        for w, h in TERMS:
                            for c in range(KC):
                                mm = pe.matmul(ps[:, n % 8, 0:WB], h[:, c, n * P:(n + 1) * P], w[:, half, c, :],
                                               start=k == 0, stop=k == 23)
                                k += 1
                        mm.then_inc(filled, 1)


def attend(nc, io, keep, scratch, sem):
    ROWS = [1, 3, 5, 7, 9, 11, 13, 15, 14, 12, 10, 8, 6, 4, 2, 0]
    SCALE = HALF ** -0.5
    NEAR = 2 * P
    WIDE = 1024
    PAIRS = HEADS // 2
    RING = 4
    AHEAD = RING - 1
    Q_RING = 4

    def pieces(i):
        w = (i + 1) * P
        return [(0, w)] if w <= WIDE else [(0, w - WIDE), (w - WIDE, WIDE)]

    NR = 2 * TILES
    rows = [(x // TILES, ROWS[x % TILES]) for x in range(NR + Q_RING)]
    chunks, groups, parts, n_c, n_g, n_r = [], [], [], 0, 0, [0]
    for half, i in rows:
        cs = []
        for m in range(2):
            for k0, w in pieces(i):
                cs.append((n_c, m, k0, w))
                n_c += 1
        gs = []
        for g in range(i // 4 + 1):
            gs.append((n_g, 4 * g, min(4 * g + 4, i + 1)))
            n_g += 1
        chunks.append(cs)
        parts.append([(m, k0, min(WIDE, (i + 1) * P - k0)) for m in range(2) for k0 in range(0, (i + 1) * P, WIDE)])
        n_r.append(n_r[-1] + len(parts[-1]))
        groups.append(gs)
    n_c, n_g, n_p = chunks[NR][0][0], groups[NR][0][0], n_r[NR]
    shared = [r for r in range(NR) if rows[r][1] >= 2]
    NS = len(shared)

    def cut(i):
        return (i + 1) * P if i < 2 else ((i + 1) * POOL_NOT) // 100 * P + (P if ((i + 1) * POOL_NOT) % 100 else 0)

    def steps(eng, run):
        run(0, -AHEAD, 0, NR)
        with eng.Fori(0, PAIRS - 1) as it:
            run(it, 0, NR, NR + AHEAD)
        run(PAIRS - 1, 0, NR, NR)

    def order(r, end):
        a = [("S", c) for c in chunks[r + AHEAD]] if r + AHEAD < end else []
        b = []
        if r >= 0:
            before = (r - 1, groups[r - 1][-1]) if r else None
            for g in groups[r]:
                b.append(("T", g))
                if before:
                    b.append(("V", before))
                before = (r, g)
            if r == NR - 1:
                b.append(("V", before))
        out = []
        while a or b:
            if a:
                out.append(a.pop(0))
            if b:
                out.append(b.pop(0))
            if len(b) > 2 * len(a) and b:
                out.append(b.pop(0))
        return out

    with ExitStack() as ctx:
        def sb(name, shape, dt=F32):
            return ctx.enter_context(nc.sbuf_tensor(name, shape, dt))

        q_st = sb("q_st", [P, Q_RING, 2, P], F32R)
        k_hi = sb("k_hi", [P, 2, 2, SEQ], F32R)
        k_lo = sb("k_lo", [P, 2, 2, SEQ], F32R)
        v_hl = sb("v_hl", [P, 2, TILES, 2 * P], F32R)
        near = sb("near", [P, 2, NEAR])
        prob = sb("prob", [P, RING, 2, SEQ])
        aT_hi = sb("aT_hi", [P, 4, 512], F32R)
        aT_lo = sb("aT_lo", [P, 4, 512], F32R)
        top = sb("top", [P, 2, 2, 3])
        peak = sb("peak", [P, 2, 2])
        shift = sb("shift", [P, 4, 2])
        sums = sb("sums", [P, 4, 2, 2])
        total = sb("total", [P, 4, 2])
        inv = sb("inv", [P, 4, 2])
        coef = sb("coef", [P, 4, 1])
        part = sb("part", [P, 2, P])
        o_sb = sb("o_sb", [P, 2, P])
        lq = sb("lq", [P, 4, HALF])
        dots = sb("dots", [P, 2])
        nil = sb("nil", [P, D // 4])
        edots = sb("edots", [P, 2])
        neg_lam = sb("neg_lam", [P, 1])
        flip = sb("flip", [P, P])
        z = sb("z", [HEADS, 3 * P])
        z0 = sb("z0", [HEADS, 1])
        onehot = sb("onehot", [32, 3 * P])
        table = sb("table", [32, HEADS])
        ps_s = ctx.enter_context(nc.psum_tensor("ps_s", [P, 2, WIDE], F32))
        ps_t = ctx.enter_context(nc.psum_tensor("ps_t", [P, 2, 512], F32))
        ps_o = ctx.enter_context(nc.psum_tensor("ps_o", [P, 2, 512], F32))
        ident = keep["ident"]
        s = lambda name: sem("b_" + name)
        head_in = [s("head_in0"), s("head_in1")]
        scored, taken, shifted, raised = s("scored"), s("taken"), s("shifted"), s("raised")
        peaked, totalled, inverted, coefed = s("peaked"), s("totalled"), s("inverted"), s("coefed")
        q_in = [s(f"q_in{k}") for k in range(Q_RING)]
        scaled, mixed_v, mixed_p = s("scaled"), s("mixed_v"), s("mixed_p")
        turned, t_hi, t_lo, summed = s("turned"), s("t_hi"), s("t_lo"), s("summed")
        parted, o_set = s("parted"), s("o_set")
        o_out = [s("o_out0"), s("o_out1")]
        tab_in, z_set, moved, flipped = (
            s("tab_in"), s("z_set"), s("moved"), s("flipped"))
        lq_in, dotted, lam_set, flip_set = s("lq_in"), s("dotted"), s("lam_set"), s("flip_set")
        nil_set, nil_out = s("nil_set"), s("nil_out")
        passed = sem("passed")
        block = ctx.enter_context(nc.Block())
        TAKEN0, TURNED0, T_LO0, SUMMED0, O_SET0, O_OUT0 = 2, 1, 2, 4, 2, 1
        skewed, unskewed = prob[:, 2, 0, :], prob[:, 2, 1, :]

        def load_kv(eng, h, buf):
            sm = head_in[buf]
            for m in range(2):
                for k_op, hl in ((k_hi, 0), (k_lo, 1)):
                    for lanes in (slice(0, HALF), slice(HALF, P)):
                        eng.dma_start(k_op[lanes, buf, m, :].bitcast(F32),
                                      scratch["qk"][bass.ds(h + HEADS, 1), hl, m * HALF:(m + 1) * HALF, :]
                                      .rearrange("o p t -> (o p) t")).then_inc(sm, 16)
            eng.dma_start(v_hl[:, buf].bitcast(F32),
                          scratch["v"][bass.ds(h, 1)].rearrange("o t p e -> p (o t) e")).then_inc(sm, 16)

        def load_near(eng, h, buf):
            eng.dma_start(near[:, buf, :],
                          scratch["near"][bass.ds(h, 1)].rearrange("o p c -> (o p) c")).then_inc(head_in[buf], 16)

        @block.sync
        def _(sp):
            sp.dma_start(table[:, :], io["rel_bias_table"]).then_inc(tab_in, 16)
            sp.dma_start(onehot[:, :], io["bucket_of_distance"]).then_inc(tab_in, 16)
            sp.dma_start(lq[:, :, :], io["diff_lambda_qk"].rearrange("o a d -> o (a d)").to_broadcast([P, 4 * HALF])
                         .rearrange("p (a d) -> p a d", a=4)).then_inc(lq_in, 16)

            qk = scratch["qk"]

            def load_q(it, r):
                half, i = rows[r]
                if r >= Q_RING:
                    gate(sp, taken, it * n_c + (chunks[r - Q_RING][-1][0] + 1 + TAKEN0), passed)
                for hl in range(2):
                    sp.dma_start(q_st[hl * HALF:(hl + 1) * HALF, r % Q_RING, :, :].bitcast(F32),
                                 qk[bass.ds(it * 2 + half, 1), hl, :, i * P:(i + 1) * P]
                                 .rearrange("o (m d) t -> d (o m) t", m=2)).then_inc(q_in[r % Q_RING], 16)

            sp.wait_ge(z_set, 3)
            sp.dma_start(scratch["z"], z[:, :]).then_inc(moved, 16)
            sp.wait_ge(moved, 16)
            zt = scratch["z"]
            sp.dma_start(skewed.rearrange("p (h c) -> p h c", h=HEADS),
                         bass.AP(tensor=zt.tensor, offset=0, ap=[[1, P], [3 * P, HEADS], [1, NEAR]])).then_inc(tab_in, 16)
            sp.wait_ge(z_set, 7)
            sp.dma_start(scratch["near"].rearrange("h p c -> p h c"),
                         unskewed.rearrange("p (h c) -> p h c", h=HEADS)).then_inc(moved, 16)
            sp.wait_ge(moved, 32)
            load_near(sp, 0, 0)

            for r in range(Q_RING):
                load_q(0, r)
            sp.wait_ge(nil_set, 1)
            spare = scratch["y"].rearrange("(b p) d -> b p d", p=P)[EXPERTS:]
            PER_PAIR = (BLOCKS_MAX - EXPERTS) // PAIRS
            EVERY = (NR - Q_RING) // PER_PAIR

            def pair(it, more):
                for r in range(Q_RING, NR + (Q_RING if more else 0)):
                    load_q(it, r)
                    n = (r - Q_RING) // EVERY
                    if (r - Q_RING) % EVERY == 0 and n < PER_PAIR:
                        sp.dma_start(spare[bass.ds(it * PER_PAIR + n, 1)]
                                     .rearrange("o p (k d) -> (o p) k d", k=4),
                                     nil[:, :].unsqueeze(1).to_broadcast([P, 4, D // 4])).then_inc(nil_out, 16)
                    if r == 5:
                        gate(sp, summed, it * n_g + SUMMED0, passed)
                        load_kv(sp, it * 2 + 1, 1)
                        load_near(sp, it * 2 + 1, 1)
                    if r == TILES + 5 and more:
                        gate(sp, summed, it * n_g + (groups[TILES - 1][-1][0] + 1 + SUMMED0), passed)
                        load_kv(sp, it * 2 + 2, 0)
                        load_near(sp, it * 2 + 2, 0)
                    elif r == TILES + 5:
                        sp.dma_start(keep["wo_raw"][:, :, :], io["diff_w_out"].rearrange("o (c p) n -> p (o c) n", p=P)
                                     [:, 0:KC // 2]).then_inc(s("wo_in"), 16)

            with sp.Fori(0, PAIRS - 1) as it:
                pair(it, True)
            pair(PAIRS - 1, False)
            sp.wait_ge(nil_out, 16 * (BLOCKS_MAX - EXPERTS))

        @block.gpsimd
        def _(pool):
            pool.memset(nil[:, :], 0.0).then_inc(nil_set, 1)
            pool.memset(flip[:, :], 1.0).then_inc(flip_set, 1)
            pool.wait_ge(flip_set, 1)
            pool.affine_select(out=flip[:, :], in_=flip[:, :], compare_op=ALU.is_equal, fill=0.0, base=-(P - 1),
                               pattern=[[1, P]], channel_multiplier=1).then_inc(flip_set, 1)
            with pool.Fori(0, PAIRS) as it:
                for n, r in enumerate(shared):
                    i = rows[r][1]
                    x, w = cut(i), (i + 1) * P
                    p0, p1 = prob[:, r % RING, 0, x:w], prob[:, r % RING, 1, x:w]
                    gate(pool, coefed, it * NR + (r + 1), passed)
                    pool.tensor_scalar(p1, p1, coef[:, r % 4, :], 0.0, ALU.mult, ALU.add).then_inc(scaled, 1)
                    pool.wait_ge(scaled, it * NS + (n + 1))
                    pool.tensor_tensor(p0, p0, p1, ALU.add).then_inc(mixed_p, 1)

        @block.scalar
        def _(act):
            load_kv(act, 0, 0)
            act.wait_ge(dotted, 2)
            nc.scalar.activation(edots[:, :], dots[:, :], ACT.Exp).then_inc(lam_set, 1)

            def raise_(it, r, m, k0, w):
                if m == 0 and k0 == 0:
                    act.wait_ge(peaked, it * NR + (r + 1))
                    nc.scalar.activation(shift[:, r % 4, :], peak[:, r % 2, :], ACT.Copy, scale=-SCALE).then_inc(shifted, 1)
                    act.wait_ge(shifted, it * NR + (r + 1))
                nc.scalar.activation(prob[:, r % RING, m, k0:k0 + w], prob[:, r % RING, m, k0:k0 + w], ACT.Exp,
                                     bias=shift[:, r % 4, m:m + 1], scale=SCALE,
                                     accum_out=sums[:, r % 4, m, (1 if k0 else 0):(2 if k0 else 1)]).then_inc(raised, 1)

            def store(it, r):
                half, i = rows[r]
                act.wait_ge(o_set, it * NR + (r + 1 + O_SET0))
                act.dma_start(scratch["o"][i * P:(i + 1) * P, bass.ds((it * 2 + half) * P, P)],
                              o_sb[:, r % 2, :]).then_inc(o_out[r % 2], 16)

            def out(it, r):
                act.wait_ge(summed, it * n_g + (groups[r][-1][0] + 1 + SUMMED0))
                act.wait_ge(o_set, it * NR + (r - 1 + O_SET0))
                nc.scalar.activation(part[:, r % 2, :], ps_o[:, r % 2, P:2 * P], ACT.Copy,
                                     scale=inv[:, r % 4, 0:1]).then_inc(parted, 1)


            def run(it, first, behind, end):
                for r in range(first, behind):
                    waiting = list(parts[r + 2]) if 0 <= r + 2 < end else []
                    turns = [what for kind, what in order(r, end) if kind == "T"]
                    for n_t, (g, k0, k1) in enumerate(turns):
                        act.wait_ge(turned, it * n_g + (g + 1 + TURNED0))
                        act.wait_ge(summed, it * n_g + (g - 3 + SUMMED0))
                        n = (k1 - k0) * P
                        nc.scalar.activation(aT_hi[:, g % 4, 0:n], ps_t[:, g % 2, 0:n], ACT.Copy).then_inc(t_hi, 1)
                        if n_t == 0 and r - 1 >= 0:
                            out(it, r - 1)
                        while waiting and len(waiting) * len(turns) > (len(turns) - n_t - 1) * len(parts[r + 2]):
                            raise_(it, r + 2, *waiting.pop(0))
                    for what in waiting:
                        raise_(it, r + 2, *what)
                    if r - 1 >= 0:
                        store(it, r - 1)
                    if r == NR - 1:
                        out(it, r)
                        store(it, r)

            steps(act, run)
            for k in range(2):
                act.wait_ge(o_out[k], 16 * PAIRS * NR // 2 + O_OUT0)

        @block.vector
        def _(dve):
            dve.sem_inc(taken, TAKEN0)
            dve.sem_inc(t_lo, T_LO0)
            dve.sem_inc(o_set, O_SET0)
            dve.wait_ge(flipped, 1)
            nc.vector.tensor_copy(z0[:, :], ps_t[0:HEADS, 0, 0:1]).then_inc(z_set, 1)
            dve.wait_ge(z_set, 1)
            nc.vector.tensor_scalar(z[:, :], ps_t[0:HEADS, 0, 0:3 * P], z0[:, 0:1], 1.0 / SCALE,
                                    ALU.subtract, ALU.mult).then_inc(z_set, 1)
            dve.wait_ge(z_set, 2)
            nc.vector.memset(z[:, NEAR:3 * P], NEG).then_inc(z_set, 1)
            dve.wait_ge(lq_in, 16)
            for k in range(2):
                nc.vector.tensor_tensor_reduce(lq[:, 2 * k, :], lq[:, 2 * k, :], lq[:, 2 * k + 1, :], 1.0, 0.0,
                                               ALU.mult, ALU.add, dots[:, k:k + 1]).then_inc(dotted, 1)
            dve.wait_ge(lam_set, 1)
            nc.vector.scalar_tensor_tensor(out=neg_lam[:, :], in0=edots[:, 1:2], scalar=LAMBDA_INIT,
                                           in1=edots[:, 0:1], op0=ALU.subtract, op1=ALU.subtract).then_inc(lam_set, 1)
            dve.wait_ge(flipped, 2)
            for k in range(4):
                nc.vector.tensor_copy(unskewed[:, k * 512:(k + 1) * 512],
                                      ps_s[:, k // 2, (k % 2) * 512:(k % 2 + 1) * 512]).then_inc(z_set, 1)
            dve.wait_ge(lam_set, 2)

            def take(it, r, c, m, k0, w):
                half, i = rows[r]
                last = k0 + w == (i + 1) * P
                n_near = min(w, NEAR) if last else 0
                far = w - n_near
                if m == 0 and k0 == 0 and r >= RING:
                    dve.wait_ge(turned, it * n_g + (groups[r - RING][-1][0] + 1 + TURNED0))
                elif m == 0 and k0 == 0:
                    dve.wait_ge(turned, it * n_g + TURNED0)
                if far:
                    dve.wait_ge(scored, it * n_c + (c + 1))
                    col = 0 if not last else 1
                    ins = nc.vector.tensor_scalar(prob[:, r % RING, m, k0:k0 + far], ps_s[:, c % 2, 0:far], 1.0, None,
                                                  ALU.mult, ALU.max, accum_out=top[:, r % 2, m, col:col + 1])
                else:
                    gate(dve, scored, it * n_c + (c + 1), passed)
                if n_near:
                    ins = nc.vector.tensor_tensor_reduce(
                        prob[:, r % RING, m, k0 + far:k0 + w], ps_s[:, c % 2, far:w], near[:, half % 2, NEAR - n_near:NEAR],
                        1.0, LOWEST, ALU.add, ALU.max, top[:, r % 2, m, 2:3])
                ins.then_inc(taken, 1)

            def peaks(it, r):
                i = rows[r][1]
                first = 0 if i >= 8 else 1 if i >= 2 else 2
                if r >= 2:
                    dve.wait_ge(shifted, it * NR + (r - 1))
                dve.wait_ge(taken, it * n_c + (chunks[r][-1][0] + 1 + TAKEN0))
                nc.vector.tensor_reduce(peak[:, r % 2, :], top[:, r % 2, :, first:3], AX.X, ALU.max).then_inc(peaked, 1)

            def sum_of(r):
                return total[:, r % 4, :] if rows[r][1] >= 8 else sums[:, r % 4, :, 0]

            def mix(it, r, step):
                i = rows[r][1]
                if step == 0:
                    dve.wait_ge(raised, it * n_p + n_r[r + 1])
                    if i >= 8:
                        nc.vector.tensor_reduce(total[:, r % 4, :], sums[:, r % 4, :, :], AX.X, ALU.add).then_inc(totalled, 1)
                    else:
                        dve.sem_inc(totalled, 1)
                elif step == 1:
                    dve.wait_ge(totalled, it * NR + (r + 1))
                    nc.vector.reciprocal(inv[:, r % 4, :], sum_of(r)).then_inc(inverted, 1)
                elif step == 2:
                    dve.wait_ge(inverted, it * NR + (r + 1))
                    nc.vector.scalar_tensor_tensor(out=coef[:, r % 4, :], in0=sum_of(r)[:, 0:1], scalar=neg_lam[:, 0:1],
                                                   in1=inv[:, r % 4, 1:2], op0=ALU.mult, op1=ALU.mult).then_inc(coefed, 1)
                else:
                    dve.wait_ge(coefed, it * NR + (r + 1))
                    x = cut(i)
                    p0, p1 = prob[:, r % RING, 0, 0:x], prob[:, r % RING, 1, 0:x]
                    nc.vector.scalar_tensor_tensor(out=p0, in0=p1, scalar=coef[:, r % 4, :], in1=p0,
                                                   op0=ALU.mult, op1=ALU.add).then_inc(mixed_v, 1)

            def out(it, r):
                dve.wait_ge(parted, it * NR + (r + 1))
                dve.wait_ge(o_out[r % 2], it * (16 * NR // 2) + (16 * (r // 2) + O_OUT0))
                nc.vector.scalar_tensor_tensor(out=o_sb[:, r % 2, :], in0=ps_o[:, r % 2, 0:P], scalar=inv[:, r % 4, 0:1],
                                               in1=part[:, r % 2, :], op0=ALU.mult, op1=ALU.add).then_inc(o_set, 1)

            for k in range(2):
                dve.sem_inc(o_out[k], O_OUT0)


            def run(it, first, behind, end):
                for r in range(first, behind):
                    mixing = 0 <= r + 1 < end
                    if mixing:
                        mix(it, r + 1, 0)
                    if 0 <= r + AHEAD - 1 < end:
                        peaks(it, r + AHEAD - 1)
                    if mixing:
                        mix(it, r + 1, 1)
                    for n, (kind, what) in enumerate(order(r, end)):
                        if kind == "S":
                            x = r + AHEAD
                            if what is chunks[x][0] and x % TILES == 0:
                                dve.wait_ge(head_in[x // TILES % 2], it * (16 * 10) + 16 * 10 * (x // NR + 1))
                            take(it, x, *what)
                        elif kind == "T":
                            g, k0, k1 = what
                            w = (k1 - k0) * P
                            dve.wait_ge(t_hi, it * n_g + (g + 1))
                            nc.vector.tensor_tensor(aT_lo[:, g % 4, 0:w], ps_t[:, g % 2, 0:w],
                                                    aT_hi[:, g % 4, 0:w].bitcast(F32), ALU.subtract).then_inc(t_lo, 1)
                        if mixing and n < 2:
                            mix(it, r + 1, 2 + n)
                    if r - 1 >= 0:
                        out(it, r - 1)
                    for n in range(len(order(r, end)), 2):
                        if mixing:
                            mix(it, r + 1, 2 + n)
                    if r == NR - 1:
                        out(it, r)

            steps(dve, run)

        @block.tensor
        def _(pe):
            pe.sem_inc(turned, TURNED0)
            pe.sem_inc(summed, SUMMED0)
            pe.wait_ge(tab_in, 32)
            pe.matmul(ps_t[0:HEADS, 0, 0:3 * P], table[:, :], onehot[:, :], start=True, stop=True).then_inc(flipped, 1)
            pe.wait_ge(tab_in, 48)
            pe.wait_ge(flip_set, 2)
            for k in range(4):
                mm = pe.matmul(ps_s[:, k // 2, (k % 2) * 512:(k % 2 + 1) * 512], flip[:, :],
                               skewed[:, k * 512:(k + 1) * 512], start=True, stop=True)
            mm.then_inc(flipped, 1)
            pe.wait_ge(z_set, 7)

            def run(it, first, behind, end):
                for r in range(first, behind):
                    for kind, what in order(r, end):
                        if kind == "S":
                            c, m, k0, w = what
                            x = r + AHEAD
                            half, i = rows[x]
                            if what is chunks[x][0] and x % TILES == 0:
                                pe.wait_ge(head_in[half % 2], it * (16 * 10) + 16 * 10 * (x // NR + 1))
                            if what is chunks[x][0]:
                                pe.wait_ge(q_in[x % Q_RING], it * (32 * NR // Q_RING) + 32 * (x // Q_RING + 1))
                            pe.wait_ge(taken, it * n_c + (c - 1 + TAKEN0))
                            for j in range(0, w, 512):
                                n = min(512, w - j)
                                for k_op in (k_lo, k_hi):
                                    mm = pe.matmul(ps_s[:, c % 2, j:j + n], q_st[:, x % Q_RING, m, :],
                                                   k_op[:, half % 2, m, k0 + j:k0 + j + n], start=k_op is k_lo,
                                                   stop=k_op is k_hi)
                            mm.then_inc(scored, 1)
                        elif kind == "T":
                            g, k0, k1 = what
                            if k0 == 0:
                                pe.wait_ge(mixed_v, it * NR + (r + 1))
                                if r in shared:
                                    pe.wait_ge(mixed_p, it * NS + (shared.index(r) + 1))
                            pe.wait_ge(t_lo, it * n_g + (g - 1 + T_LO0))
                            for k in range(k0, k1):
                                mm = pe.transpose(ps_t[:, g % 2, (k - k0) * P:(k - k0 + 1) * P],
                                                  prob[:, r % RING, 0, k * P:(k + 1) * P], ident[:, :])
                            mm.then_inc(turned, 1)
                        else:
                            x, (g, k0, k1) = what
                            half, i = rows[x]
                            pe.wait_ge(t_lo, it * n_g + (g + 1 + T_LO0))
                            if k0 == 0:
                                pe.wait_ge(o_set, it * NR + (x - 1 + O_SET0))
                            for k in range(k0, k1):
                                t = slice((k - k0) * P, (k - k0 + 1) * P)
                                pe.matmul(ps_o[:, x % 2, 0:2 * P], aT_hi[:, g % 4, t], v_hl[:, half, k, :],
                                          start=k == 0, stop=False)
                                mm = pe.matmul(ps_o[:, x % 2, 0:P], aT_lo[:, g % 4, t], v_hl[:, half, k, 0:P],
                                               start=False, stop=k == i)
                            mm.then_inc(summed, 1)

            steps(pe, run)


EXPERTS = 32
GROUPS_E = 4
PER_GROUP = EXPERTS // GROUPS_E
FF = 512
FC = FF // P
ROUTES = GROUPS_E + EXPERTS
SLOTS = EXPERTS * SEQ + P
BLOCKS_MAX = 2 * SEQ // P + EXPERTS
COLS = 7

GS, DS = 4, 2
GC, DC = KC // GS, FC // DS


def expert_rows(w, e, j, n):
    r = w.rearrange("o e (c p) n -> p (o e) c n", p=P)
    return r[:, bass.ds(e, 1), j * n:(j + 1) * n, :].rearrange("p o c n -> p (o c) n")


def load_gate_up(sp, io, raw, gu_in, e, j):
    sp.dma_start(raw[:, j, :, 0, :], expert_rows(io["moe_w_gate"], e, j, GC)).then_inc(gu_in[j], 16)
    sp.dma_start(raw[:, j, :, 1, :], expert_rows(io["moe_w_up"], e, j, GC)).then_inc(gu_in[j], 16)


def mix_and_route(nc, io, keep, scratch, sem):
    with ExitStack() as ctx:
        def sb(name, shape, dt=F32):
            return ctx.enter_context(nc.sbuf_tensor(name, shape, dt))

        wo_raw = (keep["wo_raw"], sb("wo_raw_rest", [P, KC // 2, D]))
        wo_hi = sb("wo_hi", [P, KC, D], F32R)
        wo_lo = sb("wo_lo", [P, KC, D], F32R)
        o_t = sb("o_t", [P, 2, D])
        sq = sb("sq", [P, D])
        sq2 = sb("sq2", [P, D])
        oT_hi = sb("oT_hi", [P, 2, D], F32R)
        oT_lo = sb("oT_lo", [P, 2, D], F32R)
        x2 = sb("x2", [P, 2, D])
        h2 = sb("h2", [P, 2, D])
        h2T = sb("h2T", [P, D])
        g2_row = sb("g2_row", [P, D])
        w_r = sb("w_r", [P, KC, ROUTES])
        b_r = sb("b_r", [P, ROUTES])
        sub_g = sb("sub_g", [P, 1])
        sub_gs = sb("sub_gs", [P, 1])
        eps5, eps6 = sb("eps5", [P, 1]), sb("eps6", [P, 1])
        ssh, rth, rih = sb("ssh", [P, HEADS]), sb("rth", [P, HEADS]), sb("rih", [P, HEADS])
        ss2, rt2, ri2 = sb("ss2", [P, 1]), sb("rt2", [P, 1]), sb("ri2", [P, 1])
        lg = sb("lg", [P, 8])
        le = sb("le", [P, EXPERTS])
        gm, gi = sb("gm", [P, 8]), sb("gi", [P, 8], U32)
        gf, g8 = sb("gf", [P, 1]), sb("g8", [P, 1])
        gmask = sb("gmask", [P, GROUPS_E])
        em = sb("em", [P, EXPERTS])
        es = sb("es", [P, PER_GROUP])
        ev, ei = sb("ev", [P, 8]), sb("ei", [P, 8], U32)
        ef = sb("ef", [P, 2])
        eid = sb("eid", [P, 2, 2])
        own = sb("own", [P, 2, 2, EXPERTS])
        both = sb("both", [P, 2, EXPERTS])
        before = sb("before", [P, EXPERTS])
        rank = sb("rank", [P, 2, 2])
        junk = sb("junk", [P, 2, EXPERTS])
        slot_f, slot = sb("slot_f", [P, 2]), sb("slot", [P, 2, 2], I32)
        tok_f, tok = sb("tok_f", [P, 1]), sb("tok", [P, 2], I32)
        iota_e, iota_ef = sb("iota_e", [P, EXPERTS], I32), sb("iota_ef", [P, EXPERTS])
        iota_p, iota_pf = sb("iota_p", [P, 1], I32), sb("iota_pf", [P, 1])
        ones, tri = sb("ones", [P, P]), sb("tri", [P, P])
        zeros = sb("zeros", [P, SLOTS // P], I32)
        cnt_i, nb_i = sb("cnt_i", [P, EXPERTS], I32), sb("nb_i", [P, EXPERTS], I32)
        nb, upto = sb("nb", [P, EXPERTS]), sb("upto", [P, EXPERTS])
        one_e = sb("one_e", [P, EXPERTS])
        cmp = sb("cmp", [P, EXPERTS])
        tabf, tabi = sb("tabf", [P, COLS]), sb("tabi", [P, COLS], I32)
        ps_a = ctx.enter_context(nc.psum_tensor("ps_a", [P, D], F32))
        ps_b = ctx.enter_context(nc.psum_tensor("ps_b", [P, D], F32))
        ps_c = ctx.enter_context(nc.psum_tensor("ps_c", [P, D], F32))
        ps_d = ctx.enter_context(nc.psum_tensor("ps_d", [P, 512], F32))
        ps_e = ctx.enter_context(nc.psum_tensor("ps_e", [P, 512], F32))
        ident, start, kept, e_all, rank_all = (keep[k] for k in ("ident", "start", "kept", "e_all", "rank_all"))
        s = lambda name: sem("c_" + name)
        wo_in = (sem("b_wo_in"), s("wo_in"))
        wo_hi_set, wo_split = s("wo_hi_set"), s("wo_split")
        o_in = [s("o_in0"), s("o_in1")]
        x_in = [s("x_in0"), s("x_in1")]
        const_in, made, gain_in, gain_set, index_set = (
            s("const_in"), s("made"), s("gain_in"), s("gain_set"), s("index_set"))
        squared, summed, rooted, inverted, normed = (s(n) for n in ("squared", "summed", "rooted", "inverted", "normed"))
        turned, oT_hi_set, oT_lo_set, projected, x2_set = (s(n) for n in ("turned", "oT_hi", "oT_lo", "projected", "x2"))
        squared2, rooted2, inverted2, h2_set = (s(n) for n in ("squared2", "rooted2", "inverted2", "h2"))
        x2_out, h2_out = [s("x2_out0"), s("x2_out1")], [s("h2_out0"), s("h2_out1")]
        turned2, h2T_set, routed, chosen, both_set = (s(n) for n in ("turned2", "h2T", "routed", "chosen", "both"))
        ranked, placed, slot_set, scattered, zeroed = (s(n) for n in ("ranked", "placed", "slot", "scattered", "zeroed"))
        freed, counted, tabled, tab_set = s("freed"), s("counted"), s("tabled"), s("tab_set")
        gu_in = [sem(f"d_gu_in{j}") for j in range(GS)]
        passed = sem("passed")
        block = ctx.enter_context(nc.Block())
        x_rows = io["x"].rearrange("o (t p) d -> (o t) p d", p=P)
        TURNED0, OT_LO0, PROJECTED0, X2_0, H2T0, ROUTED0, BOTH0, SLOT0, SUMMED0 = 2, 1, 2, 1, 1, 1, 1, 1, 1
        OUT0, FREED0, ROOTED2_0 = 1, 2, 1
        DEEP = 5

        def steps(eng, step, after_first=None, before_loop=None):
            for n in range(DEEP):
                step(n, n % 2, n)
                if n == 0 and after_first:
                    after_first()
            if before_loop:
                before_loop()
            pairs = (TILES - 1 - DEEP) // 2
            with eng.Fori(0, pairs) as it:
                for j in range(2):
                    step(it * 2 + (DEEP + j), (DEEP + j) % 2, DEEP)
            for n in range(DEEP + 2 * pairs, TILES + DEEP):
                step(n, n % 2, n)

        def has(at, lag):
            return 0 <= at - lag < TILES

        def uses(t, q):
            return t * 8 - 8 * q if q else t * 8

        def tile_of(dram, t):
            return dram.rearrange("(t p) d -> t p d", p=P)[bass.ds(t, 1)].rearrange("o p d -> (o p) d")

        @block.sync
        def _(sp):
            sp.dma_start(o_t[:, 0, :], tile_of(scratch["o"], 0)).then_inc(o_in[0], 16)
            sp.dma_start(sub_g[:, :], io["diff_subln"].rearrange("o p -> p o")).then_inc(gain_in, 16)
            sp.dma_start(wo_raw[1][:, :, :], io["diff_w_out"].rearrange("o (c p) n -> p (o c) n", p=P)[:, KC // 2:]
                         ).then_inc(wo_in[1], 16)
            sp.dma_start(g2_row[:, :], io["norm_ffn"].to_broadcast([P, D])).then_inc(const_in, 16)
            sp.dma_start(w_r[:, :, 0:GROUPS_E], io["moe_w_group"].rearrange("o (c p) n -> p (o c) n", p=P)).then_inc(const_in, 16)
            sp.dma_start(w_r[:, :, GROUPS_E:], io["moe_w_expert"].rearrange("o (c p) n -> p (o c) n", p=P)).then_inc(const_in, 16)
            sp.dma_start(b_r[:, 0:GROUPS_E], io["moe_b_group"].to_broadcast([P, GROUPS_E])).then_inc(const_in, 16)
            sp.dma_start(b_r[:, GROUPS_E:], io["moe_b_expert"].to_broadcast([P, EXPERTS])).then_inc(const_in, 16)

            def step(n, par, at):
                if has(at, -1):
                    gate(sp, turned, n + TURNED0, passed)
                    sp.dma_start(o_t[:, 1 - par, :], tile_of(scratch["o"], n + 1)).then_inc(o_in[1 - par], 16)
                if has(at, 2):
                    t = n - 2
                    gate(sp, h2_set, t + 1, passed)
                    sp.dma_start(tile_of(scratch["x2"], t), x2[:, par, :]).then_inc(x2_out[par], 16)
                    sp.dma_start(tile_of(scratch["h2"], t), h2[:, par, :]).then_inc(h2_out[par], 16)
                if has(at, 0):
                    gate(sp, x2_out[par], uses(n, par) + OUT0, passed)
                    sp.dma_start(x2[:, par, :], x_rows[bass.ds(n, 1)].rearrange("o p d -> (o p) d")).then_inc(x_in[par], 16)

            steps(sp, step, before_loop=lambda: [load_gate_up(sp, io, keep["gu_raw"], gu_in, 0, j) for j in range(GS)])
            for k in range(2):
                sp.wait_ge(x2_out[k], 8 * TILES + OUT0)
                sp.wait_ge(h2_out[k], 8 * TILES + OUT0)
            sp.wait_ge(tab_set, 1)
            sp.dma_start(scratch["tab"], tabi[:, :]).then_inc(tab_set, 16)
            sp.wait_ge(tab_set, 17)

        @block.gpsimd
        def _(pool):
            pool.memset(zeros[:, :], 0).then_inc(made, 1)
            pool.memset(ones[:, :], 1.0).then_inc(made, 1)
            pool.memset(one_e[:, :], 1.0).then_inc(made, 1)
            pool.memset(before[:, :], 0.0).then_inc(made, 1)
            pool.memset(lg[:, :], LOWEST).then_inc(made, 1)
            pool.memset(eps5[:, :], 1e-5).then_inc(made, 1)
            pool.memset(eps6[:, :], 1e-6).then_inc(made, 1)
            pool.iota(iota_e[:, :], pattern=[[1, EXPERTS]], base=0, channel_multiplier=0).then_inc(made, 1)
            pool.iota(iota_p[:, :], pattern=[[0, 1]], base=0, channel_multiplier=1).then_inc(made, 1)
            pool.wait_ge(made, 9)
            pool.affine_select(out=tri[:, :], in_=ones[:, :], compare_op=ALU.is_gt, fill=0.0, base=0,
                               pattern=[[1, P]], channel_multiplier=-1).then_inc(made, 1)
            pool.dma_start(scratch["slots"].rearrange("(p n) o -> p (n o)", p=P), zeros[:, :]).then_inc(zeroed, 16)
            pool.wait_ge(zeroed, 16)

            def step(n, par, at):
                if has(at, 5):
                    t, q = n - 5, 1 - par
                    gate(pool, slot_set, t + (1 + SLOT0), passed)
                    for k in range(2):
                        pool.indirect_dma_start(scratch["slots"], bass.IndirectOffsetOnAxis(ap=slot[:, q, k:k + 1], axis=0),
                                                tok[:, q:q + 1], None).then_inc(scattered, 16)
                    gate(pool, scattered, t * 32 + 32, passed)
                    pool.sem_inc(freed, 1)

            steps(pool, step)

        @block.scalar
        def _(act):
            act.sem_inc(rooted2, ROOTED2_0)
            act.wait_ge(gain_set, 1)
            act.wait_ge(made, 9)

            def step(n, par, at):
                if has(at, 2):
                    t = n - 2
                    act.wait_ge(x2_set, t + (1 + X2_0))
                    act.wait_ge(rooted2, t + ROOTED2_0)
                    nc.scalar.activation(sq2[:, :], x2[:, par, :], ACT.Square, accum_out=ss2[:, :]).then_inc(squared2, 1)
                    act.wait_ge(squared2, t + 1)
                    nc.scalar.activation(rt2[:, :], ss2[:, :], ACT.Sqrt, bias=eps6[:, 0:1], scale=1.0 / D).then_inc(rooted2, 1)
                if has(at, 0):
                    act.wait_ge(o_in[par], uses(n, par) + 16)
                    act.wait_ge(summed, n + SUMMED0)
                    nc.scalar.activation(sq[:, :], o_t[:, par, :], ACT.Square).then_inc(squared, 1)
                    act.wait_ge(summed, n + (1 + SUMMED0))
                    nc.scalar.activation(rth[:, :], ssh[:, :], ACT.Sqrt, bias=eps5[:, 0:1], scale=1.0 / P).then_inc(rooted, 1)
                    act.wait_ge(turned, n + (1 + TURNED0))
                    act.wait_ge(projected, n + (PROJECTED0 - 1))
                    nc.scalar.activation(oT_hi[:, par, :], ps_a[:, :], ACT.Copy, scale=sub_gs[:, 0:1]).then_inc(oT_hi_set, 1)
                if has(at, 2):
                    t = n - 2
                    act.wait_ge(turned2, t + 1)
                    act.wait_ge(routed, t + ROUTED0)
                    nc.scalar.activation(h2T[:, :], ps_c[:, :], ACT.Copy).then_inc(h2T_set, 1)

            def split_high():
                for half in range(2):
                    act.wait_ge(wo_in[half], 16)
                    for c in range(KC // 2):
                        nc.scalar.activation(wo_hi[:, half * (KC // 2) + c, :], wo_raw[half][:, c, :],
                                             ACT.Copy).then_inc(wo_hi_set, 1)

            steps(act, step, after_first=split_high)

        @block.vector
        def _(dve):
            dve.sem_inc(summed, SUMMED0)
            dve.sem_inc(oT_lo_set, OT_LO0)
            dve.sem_inc(x2_set, X2_0)
            dve.sem_inc(both_set, BOTH0)
            dve.sem_inc(slot_set, SLOT0)
            dve.sem_inc(freed, FREED0)
            for k in range(2):
                dve.sem_inc(x2_out[k], OUT0)
                dve.sem_inc(h2_out[k], OUT0)
            dve.wait_ge(gain_in, 16)
            nc.vector.tensor_scalar(sub_gs[:, :], sub_g[:, :], 1.0 - LAMBDA_INIT, None, ALU.mult).then_inc(gain_set, 1)
            dve.wait_ge(made, 9)
            nc.vector.tensor_copy(iota_ef[:, :], iota_e[:, :]).then_inc(index_set, 1)
            nc.vector.tensor_copy(iota_pf[:, :], iota_p[:, :]).then_inc(index_set, 1)
            dve.wait_ge(index_set, 2)
            nc.vector.tensor_scalar(tok_f[:, 0:1], iota_pf[:, :], -float(P), None, ALU.add).then_inc(index_set, 1)
            dve.wait_ge(index_set, 3)

            def chain(done, first):
                k = [0]

                def link(ins, alone=False):
                    k[0] += 1
                    ins.then_inc(done, 1)
                    if alone:
                        gate(dve, done, first + k[0], passed)
                    else:
                        dve.wait_ge(done, first + k[0])
                return link

            def step(n, par, at):
                if has(at, 2):
                    t = n - 2
                    dve.wait_ge(x_in[par], uses(t, par) + 16)
                    dve.wait_ge(projected, t + (1 + PROJECTED0))
                    nc.vector.tensor_tensor(x2[:, par, :], ps_b[:, :], x2[:, par, :], ALU.add).then_inc(x2_set, 1)
                    dve.wait_ge(rooted2, t + (1 + ROOTED2_0))
                    nc.vector.reciprocal(ri2[:, :], rt2[:, :]).then_inc(inverted2, 1)
                    dve.wait_ge(inverted2, t + 1)
                    dve.wait_ge(h2_out[par], uses(t, par) + OUT0)
                    nc.vector.scalar_tensor_tensor(out=h2[:, par, :], in0=x2[:, par, :], scalar=ri2[:, 0:1],
                                                   in1=g2_row[:, :], op0=ALU.mult, op1=ALU.mult).then_inc(h2_set, 1)
                if has(at, 0):
                    dve.wait_ge(squared, n + 1)
                    nc.vector.tensor_reduce(ssh[:, :], sq[:, :].rearrange("p (h e) -> p h e", h=HEADS), AX.X,
                                            ALU.add).then_inc(summed, 1)
                    dve.wait_ge(rooted, n + 1)
                    nc.vector.reciprocal(rih[:, :], rth[:, :]).then_inc(inverted, 1)
                    dve.wait_ge(inverted, n + 1)
                    ot = o_t[:, par, :].rearrange("p (h e) -> p h e", h=HEADS)
                    nc.vector.tensor_tensor(ot, ot, rih[:, :].unsqueeze(2).to_broadcast([P, HEADS, P]),
                                            ALU.mult).then_inc(normed, 1)
                if has(at, 4):
                    choose(n - 4, par)
                if has(at, 5):
                    place(n - 5, 1 - par)
                if has(at, 0):
                    dve.wait_ge(oT_hi_set, n + 1)
                    nc.vector.scalar_tensor_tensor(out=oT_lo[:, par, :], in0=ps_a[:, :], scalar=sub_gs[:, 0:1],
                                                   in1=oT_hi[:, par, :].bitcast(F32), op0=ALU.mult,
                                                   op1=ALU.subtract).then_inc(oT_lo_set, 1)

            def choose(t, q):
                link = chain(chosen, t * 14)
                dve.wait_ge(routed, t + (1 + ROUTED0))
                nc.vector.tensor_tensor(lg[:, 0:GROUPS_E], ps_d[:, 0:GROUPS_E], b_r[:, 0:GROUPS_E], ALU.add)
                link(nc.vector.tensor_tensor(le[:, :], ps_d[:, GROUPS_E:ROUTES], b_r[:, GROUPS_E:], ALU.add), True)
                link(nc.vector.max(gm[:, :], lg[:, :]), True)
                link(nc.vector.max_index(gi[:, :], gm[:, :], lg[:, :]))
                link(nc.vector.tensor_copy(gf[:, :], gi[:, 0:1]))
                nc.vector.tensor_scalar(g8[:, :], gf[:, :], float(PER_GROUP), None, ALU.mult)
                link(nc.vector.tensor_scalar(gmask[:, :], iota_ef[:, 0:GROUPS_E], gf[:, 0:1], None, ALU.is_equal))
                by_group = lambda a: a.rearrange("p (g j) -> p g j", g=GROUPS_E)
                link(nc.vector.tensor_tensor(by_group(em[:, :]), by_group(le[:, :]),
                                             gmask[:, :].unsqueeze(2).to_broadcast([P, GROUPS_E, PER_GROUP]), ALU.mult))
                link(nc.vector.tensor_reduce(es[:, :], em[:, :].rearrange("p (g j) -> p j g", g=GROUPS_E), AX.X, ALU.add), True)
                link(nc.vector.max(ev[:, :], es[:, :]), True)
                link(nc.vector.max_index(ei[:, :], ev[:, :], es[:, :]))
                link(nc.vector.tensor_copy(ef[:, :], ei[:, 0:2]))
                link(nc.vector.tensor_scalar(eid[:, q, :], ef[:, :], g8[:, 0:1], None, ALU.add))
                link(nc.vector.tensor_scalar(own[:, q, 0, :], iota_ef[:, :], eid[:, q, 0:1], None, ALU.is_equal))
                link(nc.vector.tensor_scalar(own[:, q, 1, :], iota_ef[:, :], eid[:, q, 1:2], None, ALU.is_equal))
                nc.vector.tensor_copy(kept[:, bass.ds(t, 1), 0:4].rearrange("p o n -> p (o n)"), lg[:, 0:4])
                nc.vector.tensor_copy(kept[:, bass.ds(t, 1), 4:6].rearrange("p o n -> p (o n)"), ev[:, 0:2])
                link(nc.vector.tensor_copy(e_all[:, bass.ds(t, 1), :].rearrange("p o n -> p (o n)"), eid[:, q, :]))
                nc.vector.tensor_tensor(both[:, q, :], own[:, q, 0, :], own[:, q, 1, :], ALU.add).then_inc(both_set, 1)

            def place(t, q):
                link = chain(placed, t * 6)
                dve.wait_ge(ranked, t + 1)
                for j in range(2):
                    gate(dve, ranked, t + 1, passed)
                    link(nc.vector.tensor_tensor_reduce(junk[:, j, :], own[:, q, j, :], ps_e[:, 0:EXPERTS], 1.0, 0.0,
                                                        ALU.mult, ALU.add, rank[:, q, j:j + 1]))
                nc.vector.tensor_copy(rank_all[:, bass.ds(t, 1), :].rearrange("p o n -> p (o n)"), rank[:, q, :])
                link(nc.vector.scalar_tensor_tensor(out=slot_f[:, :], in0=eid[:, q, :], scalar=float(SEQ),
                                                    in1=rank[:, q, :], op0=ALU.mult, op1=ALU.add))
                link(nc.vector.tensor_scalar(tok_f[:, 0:1], tok_f[:, 0:1], float(P), None, ALU.add))
                dve.wait_ge(freed, t + (FREED0 - 1))
                link(nc.vector.tensor_copy(tok[:, q:q + 1], tok_f[:, 0:1]))
                link(nc.vector.tensor_tensor(before[:, :], before[:, :], both[:, q, :], ALU.add))
                nc.vector.tensor_copy(slot[:, q, :], slot_f[:, :]).then_inc(slot_set, 1)

            def split_low():
                for c in range(KC):
                    dve.wait_ge(wo_hi_set, c + 1)
                    nc.vector.tensor_tensor(wo_lo[:, c, :], wo_raw[2 * c // KC][:, c % (KC // 2), :], wo_hi[:, c, :].bitcast(F32),
                                            ALU.subtract).then_inc(wo_split, 1)
                dve.wait_ge(const_in, 16 * 5)

            steps(dve, step, after_first=split_low)

            link = chain(tabled, 0)
            dve.wait_ge(counted, 1)
            link(nc.vector.tensor_scalar(cnt_i[:, :], ps_e[:, 0:EXPERTS], float(P - 1), None, ALU.add))
            link(nc.vector.tensor_scalar(nb_i[:, :], cnt_i[:, :], P.bit_length() - 1, None, ALU.logical_shift_right))
            link(nc.vector.tensor_scalar(nb[:, :], nb_i[:, :], 1.0, None, ALU.max))
            link(nc.vector.tensor_tensor_scan(upto[:, :], one_e[:, :], nb[:, :], 0.0, ALU.mult, ALU.add))
            link(nc.vector.tensor_tensor(start[:, :], upto[:, :], nb[:, :], ALU.subtract))
            nc.vector.tensor_copy(tabf[:, 4:5], upto[:, EXPERTS - 1:EXPERTS])
            link(nc.vector.tensor_scalar(cmp[:, :], start[:, :], iota_pf[:, 0:1], None, ALU.is_le))
            link(nc.vector.tensor_reduce(tabf[:, 0:1], cmp[:, :], AX.X, ALU.add))
            link(nc.vector.tensor_tensor(cmp[:, :], cmp[:, :], start[:, :], ALU.mult))
            link(nc.vector.tensor_reduce(tabf[:, 5:6], cmp[:, :], AX.X, ALU.max))
            link(nc.vector.tensor_scalar(cmp[:, :], start[:, :], iota_pf[:, 0:1], None, ALU.is_equal))
            link(nc.vector.tensor_reduce(tabf[:, 3:4], cmp[:, :], AX.X, ALU.max))
            link(nc.vector.tensor_scalar(cmp[:, :], start[:, :], iota_pf[:, 0:1], 1.0, ALU.subtract, ALU.is_equal))
            link(nc.vector.tensor_reduce(tabf[:, 2:3], cmp[:, :], AX.X, ALU.max))
            link(nc.vector.tensor_scalar(tabf[:, 0:1], tabf[:, 0:1], -1.0, None, ALU.add))
            link(nc.vector.tensor_tensor(tabf[:, 6:7], iota_pf[:, 0:1], tabf[:, 5:6], ALU.subtract))
            link(nc.vector.tensor_scalar(tabf[:, 6:7], tabf[:, 6:7], float(P), None, ALU.mult))
            link(nc.vector.scalar_tensor_tensor(out=tabf[:, 1:2], in0=tabf[:, 0:1], scalar=float(SEQ), in1=tabf[:, 6:7],
                                                op0=ALU.mult, op1=ALU.add))
            nc.vector.tensor_copy(tabi[:, :], tabf[:, :]).then_inc(tab_set, 1)

        @block.tensor
        def _(pe):
            pe.sem_inc(turned, TURNED0)
            pe.sem_inc(projected, PROJECTED0)
            pe.sem_inc(routed, ROUTED0)
            pe.sem_inc(h2T_set, H2T0)
            pe.wait_ge(made, 10)

            def step(n, par, at):
                if has(at, 1):
                    t, q = n - 1, 1 - par
                    pe.wait_ge(oT_lo_set, t + (1 + OT_LO0))
                    pe.wait_ge(x2_set, t + X2_0)
                    k = 0
                    for o, w in ((oT_lo, wo_hi), (oT_hi, wo_lo), (oT_hi, wo_hi)):
                        for c in range(KC):
                            for j in range(2):
                                mm = pe.matmul(ps_b[:, j * 512:(j + 1) * 512], o[:, q, c * P:(c + 1) * P],
                                               w[:, c, j * 512:(j + 1) * 512], start=k == 0, stop=k == 23)
                            k += 1
                    mm.then_inc(projected, 1)
                if has(at, 0):
                    pe.wait_ge(normed, n + 1)
                    pe.wait_ge(oT_lo_set, n + OT_LO0)
                    for c in range(KC):
                        mm = pe.transpose(ps_a[:, c * P:(c + 1) * P], o_t[:, par, c * P:(c + 1) * P], ident[:, :])
                    mm.then_inc(turned, 1)
                if has(at, 2):
                    t = n - 2
                    pe.wait_ge(h2_set, t + 1)
                    pe.wait_ge(h2T_set, t + H2T0)
                    for c in range(KC):
                        mm = pe.transpose(ps_c[:, c * P:(c + 1) * P], h2[:, par, c * P:(c + 1) * P], ident[:, :])
                    mm.then_inc(turned2, 1)
                if has(at, 3):
                    t = n - 3
                    pe.wait_ge(h2T_set, t + (1 + H2T0))
                    pe.wait_ge(both_set, t + BOTH0)
                    for c in range(KC):
                        mm = pe.matmul(ps_d[:, 0:ROUTES], h2T[:, c * P:(c + 1) * P], w_r[:, c, :], start=c == 0,
                                       stop=c == KC - 1)
                    mm.then_inc(routed, 1)
                if has(at, 4):
                    t, q = n - 4, par
                    pe.wait_ge(both_set, t + (1 + BOTH0))
                    pe.wait_ge(slot_set, t + SLOT0)
                    pe.matmul(ps_e[:, 0:EXPERTS], ones[:, :], before[:, :], start=True, stop=False)
                    pe.matmul(ps_e[:, 0:EXPERTS], tri[:, :], both[:, q, :], start=False, stop=True).then_inc(ranked, 1)

            def weights_in():
                pe.wait_ge(wo_split, KC)
                pe.wait_ge(const_in, 16 * 5)

            steps(pe, step, after_first=weights_in)
            pe.wait_ge(slot_set, TILES + SLOT0)
            pe.matmul(ps_e[:, 0:EXPERTS], ones[:, :], before[:, :], start=True, stop=True).then_inc(counted, 1)


def run_experts(nc, io, keep, scratch, sem):
    with ExitStack() as ctx:
        def sb(name, shape, dt=F32):
            return ctx.enter_context(nc.sbuf_tensor(name, shape, dt))

        gu_raw = keep["gu_raw"]
        gu_hi = sb("gu_hi", [P, KC, 2, FF], F32R)
        gu_lo = sb("gu_lo", [P, KC, 2, FF], F32R)
        d_raw = sb("d_raw", [P, DS, DC, D])
        d_hi = sb("d_hi", [P, FC, D], F32R)
        d_lo = sb("d_lo", [P, FC, D], F32R)
        table = sb("block_table", [1, P * COLS], I32)
        listed = sb("listed", [P, 1], I32)
        xg = sb("xg", [P, D])
        xT_hi, xT_lo = sb("xT_hi", [P, D], F32R), sb("xT_lo", [P, D], F32R)
        act_g = sb("act_g", [P, FF])
        hid = sb("hid", [P, FF])
        hT_hi, hT_lo = sb("hT_hi", [P, FF], F32R), sb("hT_lo", [P, FF], F32R)
        y_sb = sb("y_sb", [P, D])
        own = sb("own_all", [P, 2 * TILES, EXPERTS])
        first_row = sb("first_row", [P, 2 * TILES])
        iota_i, iota_f = sb("iota_i4", [P, EXPERTS], I32), sb("iota_f4", [P, EXPERTS])
        dest_f = sb("dest_f", [P, 2 * TILES])
        ps_x = ctx.enter_context(nc.psum_tensor("ps_x", [P, D], F32))
        ps_g = ctx.enter_context(nc.psum_tensor("ps_g", [P, 2, FF], F32))
        ps_h = ctx.enter_context(nc.psum_tensor("ps_h", [P, FF], F32))
        ps_y = ctx.enter_context(nc.psum_tensor("ps_y", [P, D], F32))
        ident, start, e_all, rank_all, dest = (keep[k] for k in ("ident", "start", "e_all", "rank_all", "dest"))
        s = lambda name: sem("d_" + name)
        gu_in, d_in = [s(f"gu_in{j}") for j in range(GS)], [s(f"d_in{j}") for j in range(DS)]
        gu_hi_set, gu_split, gu_ready, gu_used = s("gu_hi"), s("gu_split"), s("gu_ready"), s("gu_used")
        d_hi_set, d_split, d_ready, d_used = s("d_hi"), s("d_split"), s("d_ready"), s("d_used")
        table_in, listed_in, x_in, x_turned = s("table_in"), s("listed_in"), s("x_in"), s("x_turned")
        x_hi_set, x_lo_set, act_set, hid_set = s("x_hi"), s("x_lo"), s("act"), s("hid")
        h_turned, h_hi_set, h_lo_set, y_taken, y_out = s("h_turned"), s("h_hi"), s("h_lo"), s("y_taken"), s("y_out")
        iota_set, found = s("iota"), s("found")
        passed = sem("passed")
        block = ctx.enter_context(nc.Block())
        GU_SPLIT0, D_SPLIT0, D_READY0, D_USED0, X_TURNED0, Y_TAKEN0, Y_OUT0, H_LO0 = GS, DS, DS, DS, 1, 2, 17, 1
        EARLY, LATE = range(GS // 4), range(GS // 4, GS)
        COL_EXPERT, COL_LIST, COL_NEXT, COL_FIRST, COL_BLOCKS = range(5)

        def look(eng, b, column, least, most):
            return eng.value_load(table[0:1, bass.ds(b * COLS + column, 1)], min_val=least, max_val=most)

        def blocks_of(eng):
            eng.wait_ge(table_in, 16)
            return look(eng, 0, COL_BLOCKS, EXPERTS, BLOCKS_MAX - 1)

        @block.sync
        def _(sp):
            sp.dma_start(table[:, :], scratch["tab"].rearrange("(o p) c -> o (p c)", o=1)).then_inc(table_in, 16)

            def load_down(e):
                for j in range(DS):
                    gate(sp, d_split, e * DS + (j + 1), passed)
                    sp.dma_start(d_raw[:, j, :, :], expert_rows(io["moe_w_down"], e, j, DC)).then_inc(d_in[j], 16)

            with sp.Fori(0, EXPERTS - 1) as e:
                load_down(e)
                for j in range(GS):
                    gate(sp, gu_split, e * GS + (GS + j + 1), passed)
                    load_gate_up(sp, io, gu_raw, gu_in, e + 1, j)
            load_down(EXPERTS - 1)

        @block.gpsimd
        def _(pool):
            pool.iota(iota_i[:, :], pattern=[[1, EXPERTS]], base=0, channel_multiplier=0).then_inc(iota_set, 1)
            n = blocks_of(pool)
            with pool.Fori(0, n + 1) as b:
                at = look(pool, b, COL_LIST, 0, SLOTS - P)
                gate(pool, x_turned, b + X_TURNED0, passed)
                pool.dma_start(listed[:, :], scratch["slots"][bass.ds(at, P), :]).then_inc(listed_in, 16)
                gate(pool, listed_in, b * 16 + 16, passed)
                pool.indirect_dma_start(xg[:, :], None, scratch["h2"],
                                        bass.IndirectOffsetOnAxis(ap=listed[:, 0:1], axis=0)).then_inc(x_in, 16)

        @block.scalar
        def _(act):
            n = blocks_of(act)

            def gu_high(e, freed, slots):
                for j in slots:
                    if freed is not None:
                        act.wait_ge(gu_used, freed + (j + 1))
                    act.wait_ge(gu_in[j], e * 32 + 32)
                    nc.scalar.activation(gu_hi[:, j * GC:(j + 1) * GC], gu_raw[:, j], ACT.Copy).then_inc(gu_hi_set, 1)

            def d_high(e, freed):
                for j in range(DS):
                    if freed is not None:
                        act.wait_ge(d_used, freed + (j + 1))
                    act.wait_ge(d_in[j], e * 16 + 16)
                    nc.scalar.activation(d_hi[:, j * DC:(j + 1) * DC, :], d_raw[:, j], ACT.Copy).then_inc(d_hi_set, 1)

            def x_high(b):
                act.wait_ge(x_turned, b + (1 + X_TURNED0))
                nc.scalar.activation(xT_hi[:, :], ps_x[:, :], ACT.Copy).then_inc(x_hi_set, 1)

            def take_y(k):
                act.wait_ge(d_used, k * DS + D_USED0)
                act.wait_ge(y_out, k * 16 + (Y_OUT0 - 16))
                nc.scalar.activation(y_sb[:, :], ps_y[:, :], ACT.Copy).then_inc(y_taken, 1)

            def store_y(k):
                gate(act, y_taken, k + Y_TAKEN0, passed)
                act.dma_start(scratch["y"].rearrange("(b p) d -> b p d", p=P)[bass.ds(k - 1, 1)].rearrange("o p d -> (o p) d"),
                              y_sb[:, :]).then_inc(y_out, 16)

            def iteration(b, first):
                e = look(act, b, COL_EXPERT, 0, EXPERTS - 1)
                more = look(act, b, COL_NEXT, 0, 1)
                new = look(act, b, COL_FIRST, 0, 1)
                with act.If(more > 0):
                    gu_high(e + 1, b * GS, EARLY)
                act.wait_ge(gu_used, b * GS + GS)
                nc.scalar.activation(act_g[:, :], ps_g[:, 0, :], ACT.Silu).then_inc(act_set, 1)
                x_high(b + 1)
                with act.If(more > 0):
                    gu_high(e + 1, b * GS, LATE)
                if not first:
                    take_y(b)
                    with act.If(new > 0):
                        d_high(e, b * DS + (D_USED0 - DS))
                act.wait_ge(h_turned, b + 1)
                nc.scalar.activation(hT_hi[:, :], ps_h[:, :], ACT.Copy).then_inc(h_hi_set, 1)
                if not first:
                    store_y(b)

            gu_high(0, None, range(GS))
            d_high(0, None)
            x_high(0)
            iteration(0, True)
            with act.Fori(1, n) as b:
                iteration(b, False)
            take_y(n)
            store_y(n)
            act.wait_ge(y_out, n * 16 + Y_OUT0)
            act.sem_inc(passed, 1)

        @block.vector
        def _(dve):
            dve.sem_inc(gu_split, GU_SPLIT0)
            dve.sem_inc(d_split, D_SPLIT0)
            dve.sem_inc(d_ready, D_READY0)
            dve.sem_inc(h_lo_set, H_LO0)
            n = blocks_of(dve)

            def gu_low(e, slots):
                for j in slots:
                    dve.wait_ge(gu_hi_set, e * GS + (j + 1))
                    nc.vector.tensor_tensor(gu_lo[:, j * GC:(j + 1) * GC], gu_raw[:, j],
                                            gu_hi[:, j * GC:(j + 1) * GC].bitcast(F32), ALU.subtract).then_inc(gu_split, 1)
                    dve.wait_ge(gu_split, e * GS + (j + 1 + GU_SPLIT0))
                    dve.sem_inc(gu_ready, 1)

            def d_low(e):
                for j in range(DS):
                    dve.wait_ge(d_hi_set, e * DS + (j + 1))
                    nc.vector.tensor_tensor(d_lo[:, j * DC:(j + 1) * DC, :], d_raw[:, j],
                                            d_hi[:, j * DC:(j + 1) * DC, :].bitcast(F32), ALU.subtract).then_inc(d_split, 1)
                    dve.wait_ge(d_split, e * DS + (j + 1 + D_SPLIT0))
                    dve.sem_inc(d_ready, 1)

            def x_low(b):
                dve.wait_ge(x_hi_set, b + 1)
                nc.vector.tensor_tensor(xT_lo[:, :], ps_x[:, :], xT_hi[:, :].bitcast(F32), ALU.subtract).then_inc(x_lo_set, 1)

            def iteration(b, first):
                e = look(dve, b, COL_EXPERT, 0, EXPERTS - 1)
                more = look(dve, b, COL_NEXT, 0, 1)
                new = look(dve, b, COL_FIRST, 0, 1)
                with dve.If(more > 0):
                    gu_low(e + 1, EARLY)
                with dve.Else():
                    dve.sem_inc(gu_ready, len(EARLY))
                dve.wait_ge(act_set, b + 1)
                nc.vector.tensor_tensor(hid[:, :], act_g[:, :], ps_g[:, 1, :], ALU.mult).then_inc(hid_set, 1)
                x_low(b + 1)
                with dve.If(more > 0):
                    gu_low(e + 1, LATE)
                with dve.Else():
                    dve.sem_inc(gu_ready, len(LATE))
                if not first:
                    with dve.If(new > 0):
                        d_low(e)
                    with dve.Else():
                        dve.sem_inc(d_ready, DS)
                dve.wait_ge(h_hi_set, b + 1)
                nc.vector.tensor_tensor(hT_lo[:, :], ps_h[:, :], hT_hi[:, :].bitcast(F32), ALU.subtract).then_inc(h_lo_set, 1)

            gu_low(0, range(GS))
            d_low(0)
            x_low(0)
            iteration(0, True)
            with dve.Fori(1, n) as b:
                iteration(b, False)

            k = [0]

            def link(ins):
                k[0] += 1
                ins.then_inc(found, 1)
                dve.wait_ge(found, k[0])

            pairs = 2 * TILES
            dve.wait_ge(iota_set, 1)
            link(nc.vector.tensor_copy(iota_f[:, :], iota_i[:, :]))
            link(nc.vector.tensor_tensor(own[:, :, :], iota_f[:, :].unsqueeze(1).to_broadcast([P, pairs, EXPERTS]),
                                         e_all[:, :, :].rearrange("p t k -> p (t k)").unsqueeze(2)
                                         .to_broadcast([P, pairs, EXPERTS]), ALU.is_equal))
            link(nc.vector.tensor_tensor(own[:, :, :], own[:, :, :],
                                         start[:, :].unsqueeze(1).to_broadcast([P, pairs, EXPERTS]), ALU.mult))
            link(nc.vector.tensor_reduce(first_row[:, :], own[:, :, :], AX.X, ALU.add))
            link(nc.vector.scalar_tensor_tensor(out=dest_f[:, :], in0=first_row[:, :], scalar=float(P),
                                                in1=rank_all[:, :, :].rearrange("p t k -> p (t k)"),
                                                op0=ALU.mult, op1=ALU.add))
            link(nc.vector.tensor_copy(dest[:, :], dest_f[:, :]))

        @block.tensor
        def _(pe):
            pe.sem_inc(x_turned, X_TURNED0)
            pe.sem_inc(y_taken, Y_TAKEN0)
            pe.sem_inc(y_out, Y_OUT0)
            pe.sem_inc(d_used, D_USED0)
            n = blocks_of(pe)

            def turn_x(b):
                pe.wait_ge(x_in, b * 16 + 16)
                for c in range(KC):
                    mm = pe.transpose(ps_x[:, c * P:(c + 1) * P], xg[:, c * P:(c + 1) * P], ident[:, :])
                mm.then_inc(x_turned, 1)

            def gate_up(b):
                pe.wait_ge(x_lo_set, b + 1)
                for c in range(KC):
                    if c % GC == 0:
                        pe.wait_ge(gu_ready, b * GS + (c // GC + 1))
                    cs = slice(c * P, (c + 1) * P)
                    for k, (x, w) in enumerate(((xT_lo, gu_hi), (xT_hi, gu_lo), (xT_hi, gu_hi))):
                        for half in range(2):
                            mm = pe.matmul(ps_g[:, half, :], x[:, cs], w[:, c, half, :], start=c == 0 and k == 0,
                                           stop=c == KC - 1 and k == 2)
                    if c % GC == GC - 1:
                        mm.then_inc(gu_used, 1)

            def turn_h(b):
                pe.wait_ge(hid_set, b + 1)
                for f in range(FC):
                    mm = pe.transpose(ps_h[:, f * P:(f + 1) * P], hid[:, f * P:(f + 1) * P], ident[:, :])
                mm.then_inc(h_turned, 1)

            def down(k):
                pe.wait_ge(h_lo_set, k + H_LO0)
                pe.wait_ge(y_taken, k + (Y_TAKEN0 - 1))
                for f in range(FC):
                    if f % DC == 0:
                        pe.wait_ge(d_ready, k * DS + (f // DC + 1 + D_READY0 - DS))
                    fs = slice(f * P, (f + 1) * P)
                    for term, (h, w) in enumerate(((hT_lo, d_hi), (hT_hi, d_lo), (hT_hi, d_hi))):
                        for half in range(2):
                            hs = slice(half * 512, (half + 1) * 512)
                            mm = pe.matmul(ps_y[:, hs], h[:, fs], w[:, f, hs], start=f == 0 and term == 0,
                                           stop=f == FC - 1 and term == 2)
                    if f % DC == DC - 1:
                        mm.then_inc(d_used, 1)

            turn_x(0)
            gate_up(0)
            turn_x(1)
            turn_h(0)
            with pe.Fori(1, n) as b:
                gate_up(b)
                turn_x(b + 1)
                down(b)
                turn_h(b)
            down(n)


def finish(nc, io, keep, scratch, sem, out):
    RING = 4
    with ExitStack() as ctx:
        def sb(name, shape, dt=F32):
            return ctx.enter_context(nc.sbuf_tensor(name, shape, dt))

        y = sb("y_two", [P, RING, 2, D])
        acc = sb("acc", [P, RING, D])
        sq = sb("sq5", [P, D])
        g_row = sb("g5_row", [P, D])
        rows = sb("rows", [P, RING, 2], I32)
        peak = sb("peak5", [P, TILES])
        e_l = sb("e_l", [P, TILES, GROUPS_E])
        e_sum, e_v = sb("e_sum", [P, TILES]), sb("e_v", [P, TILES])
        den = sb("den", [P, TILES])
        w_all = sb("w_all", [P, 2, TILES])
        eps = sb("eps55", [P, 1])
        ss, rt, ri = sb("ss5", [P, RING]), sb("rt5", [P, RING]), sb("ri5", [P, RING])
        kept, dest = keep["kept"], keep["dest"]
        s = lambda name: sem("e_" + name)
        g_in, x_in, y_in = s("g_in"), [s(f"x_in{i}") for i in range(RING)], [s(f"y_in{i}") for i in range(RING)]
        rows_set, weigh, exped, mixed, eps_set = s("rows"), s("weigh"), s("exped"), s("mixed"), s("eps")
        added, squared, rooted, inverted, done = s("added"), s("squared"), s("rooted"), s("inverted"), s("done")
        stored = [s(f"stored{i}") for i in range(RING)]
        passed = sem("passed")
        block = ctx.enter_context(nc.Block())
        ADDED0, STORED0, SQUARED0 = RING, 1, 1
        out_rows = out.rearrange("o (t p) d -> (o t) p d", p=P)

        @block.sync
        def _(sp):
            sp.dma_start(g_row[:, :], io["norm_final"].rearrange("(o d) -> o d", o=1).to_broadcast([P, D])).then_inc(g_in, 16)

            def load(t, i):
                gate(sp, stored[i], t * 4 - 4 * i + STORED0 if i else t * 4 + STORED0, passed)
                sp.dma_start(acc[:, i, :], scratch["x2"].rearrange("(t p) d -> t p d", p=P)[bass.ds(t, 1)]
                             .rearrange("o p d -> (o p) d")).then_inc(x_in[i], 16)

            for i in range(RING):
                load(i, i)

            def store(t, i):
                gate(sp, done, t + 1, passed)
                sp.dma_start(out_rows[bass.ds(t, 1)].rearrange("o p d -> (o p) d"), acc[:, i, :]).then_inc(stored[i], 16)

            with sp.Fori(0, TILES // RING - 1) as q:
                for i in range(RING):
                    store(q * RING + i, i)
                    if i >= 1:
                        load(q * RING + (RING + i - 1), i - 1)
                load(q * RING + (2 * RING - 1), RING - 1)
            for i in range(RING):
                store(TILES - RING + i, i)
            for i in range(RING):
                sp.wait_ge(stored[i], 16 * TILES // RING + STORED0)

        @block.gpsimd
        def _(pool):
            pool.memset(eps[:, :], 1e-6).then_inc(eps_set, 1)
            with pool.Fori(0, TILES // RING) as q:
                for i in range(RING):
                    gate(pool, added, q * RING + (i + 1), passed)
                    pool.tensor_copy(rows[:, i, :], dest[:, bass.ds(q * (2 * RING) + 2 * i, 2)]).then_inc(rows_set, 1)
                    gate(pool, rows_set, q * RING + (i + 1), passed)
                    for k in range(2):
                        pool.indirect_dma_start(y[:, i, k, :], None, scratch["y"],
                                                bass.IndirectOffsetOnAxis(ap=rows[:, i, k:k + 1], axis=0)).then_inc(y_in[i], 16)

        @block.scalar
        def _(act):
            act.sem_inc(squared, SQUARED0)
            act.wait_ge(weigh, 3)
            nc.scalar.activation(e_l[:, :, :], e_l[:, :, :], ACT.Exp).then_inc(exped, 1)
            nc.scalar.activation(e_v[:, :], e_v[:, :], ACT.Exp).then_inc(exped, 1)
            act.wait_ge(eps_set, 1)
            with act.Fori(0, TILES // RING) as q:
                for i in range(RING):
                    act.wait_ge(added, q * RING + (i + 1 + ADDED0))
                    act.wait_ge(squared, q * RING + (i + SQUARED0))
                    nc.scalar.activation(sq[:, :], acc[:, i, :], ACT.Square, accum_out=ss[:, i:i + 1]).then_inc(squared, 1)
                    act.wait_ge(squared, q * RING + (i + 1 + SQUARED0))
                    nc.scalar.activation(rt[:, i:i + 1], ss[:, i:i + 1], ACT.Sqrt, bias=eps[:, 0:1],
                                         scale=1.0 / D).then_inc(rooted, 1)

        @block.vector
        def _(dve):
            for i in range(RING):
                dve.sem_inc(stored[i], STORED0)
            dve.sem_inc(added, ADDED0)
            k = [0]

            def link(ins):
                k[0] += 1
                ins.then_inc(weigh, 1)
                dve.wait_ge(weigh, k[0])

            link(nc.vector.tensor_reduce(peak[:, :], kept[:, :, 0:GROUPS_E], AX.X, ALU.max))
            link(nc.vector.tensor_tensor(e_l[:, :, :], kept[:, :, 0:GROUPS_E],
                                         peak[:, :].unsqueeze(2).to_broadcast([P, TILES, GROUPS_E]), ALU.subtract))
            link(nc.vector.tensor_tensor(e_v[:, :], kept[:, :, 5], kept[:, :, 4], ALU.subtract))
            dve.wait_ge(exped, 2)
            link(nc.vector.tensor_reduce(e_sum[:, :], e_l[:, :, :], AX.X, ALU.add))
            link(nc.vector.scalar_tensor_tensor(out=den[:, :], in0=e_v[:, :], scalar=1.0, in1=e_sum[:, :],
                                                op0=ALU.add, op1=ALU.mult))
            link(nc.vector.reciprocal(w_all[:, 0, :], den[:, :]))
            link(nc.vector.tensor_tensor(w_all[:, 1, :], w_all[:, 0, :], e_v[:, :], ALU.mult))
            dve.wait_ge(g_in, 16)

            def scale(q, i):
                dve.wait_ge(rooted, q * RING + (i + 1))
                nc.vector.reciprocal(ri[:, i:i + 1], rt[:, i:i + 1]).then_inc(inverted, 1)
                dve.wait_ge(inverted, q * RING + (i + 1))
                nc.vector.scalar_tensor_tensor(out=acc[:, i, :], in0=acc[:, i, :], scalar=ri[:, i:i + 1], in1=g_row[:, :],
                                               op0=ALU.mult, op1=ALU.mult).then_inc(done, 1)

            with dve.Fori(0, TILES // RING) as q:
                for i in range(RING):
                    dve.wait_ge(x_in[i], q * 16 + 16)
                    dve.wait_ge(y_in[i], q * 32 + 32)
                    a = acc[:, i, :]
                    nc.vector.scalar_tensor_tensor(out=a, in0=y[:, i, 0, :], scalar=w_all[:, 0, bass.ds(q * RING + i, 1)],
                                                   in1=a, op0=ALU.mult, op1=ALU.add).then_inc(mixed, 1)
                    dve.wait_ge(mixed, q * RING + (i + 1))
                    nc.vector.scalar_tensor_tensor(out=a, in0=y[:, i, 1, :], scalar=w_all[:, 1, bass.ds(q * RING + i, 1)],
                                                   in1=a, op0=ALU.mult, op1=ALU.add).then_inc(added, 1)
                    if i >= 1:
                        scale(q, i - 1)
                scale(q, RING - 1)


def build(nc, io, out):
    with ExitStack() as ctx:
        sems = {}

        def sem(name):
            if name not in sems:
                sems[name] = ctx.enter_context(nc.semaphore(name))
            return sems[name]

        def sb(name, shape, dt=F32):
            return ctx.enter_context(nc.sbuf_tensor(name, shape, dt))

        keep = {"ident": sb("ident", [P, P]), "ident_set": sem("ident_set"), "start": sb("start", [P, 32]),
                "kept": sb("kept", [P, TILES, 6]), "e_all": sb("e_all", [P, TILES, 2]),
                "rank_all": sb("rank_all", [P, TILES, 2]), "dest": sb("dest", [P, 2 * TILES], I32)}
        scratch = {
            "qk": nc.dram_tensor("qk", (2 * HEADS, 2, P, SEQ), F32).ap(),
            "v": nc.dram_tensor("v", (HEADS, TILES, P, 2 * P), F32).ap(),
            "z": nc.dram_tensor("z_rows", (HEADS, 3 * P), F32).ap(),
            "near": nc.dram_tensor("near_rows", (HEADS, P, 2 * P), F32).ap(),
            "o": nc.dram_tensor("o_rows", (SEQ, D), F32).ap(),
            "x2": nc.dram_tensor("x2_rows", (SEQ, D), F32).ap(),
            "h2": nc.dram_tensor("h2_rows", (SEQ, D), F32).ap(),
            "slots": nc.dram_tensor("slots", (SLOTS, 1), I32).ap(),
            "y": nc.dram_tensor("y_rows", (BLOCKS_MAX * P, D), F32).ap(),
            "tab": nc.dram_tensor("tab", (P, COLS), I32).ap(),
        }
        project(nc, io, keep, scratch, sem)
        keep["wo_raw"] = sb("wo_raw", [P, KC // 2, D])
        attend(nc, io, keep, scratch, sem)
        keep["gu_raw"] = sb("gu_raw", [P, GS, GC, 2, FF])
        mix_and_route(nc, io, keep, scratch, sem)
        run_experts(nc, io, keep, scratch, sem)
        finish(nc, io, keep, scratch, sem, out)


_INS = ["x", "rel_bias_table", "norm_mix", "norm_ffn", "norm_final", "diff_w_in", "diff_lambda_qk", "diff_subln",
        "diff_w_out", "moe_w_group", "moe_b_group", "moe_w_expert", "moe_b_expert", "moe_w_gate", "moe_w_up",
        "moe_w_down"]


def distance_buckets(buckets=32, most=128):
    import math
    import numpy as np

    distance = np.maximum(2 * P - 1 - np.arange(3 * P), 0)
    exact = buckets // 2
    f = np.maximum(distance, exact).astype(np.float32)
    far = exact + (np.log(f / exact) / math.log(most / exact) * (buckets - exact)).astype(np.int32)
    bucket = np.where(distance < exact, distance, np.minimum(far, buckets - 1))
    return (np.arange(buckets)[:, None] == bucket[None, :]).astype(np.float32)


def kernel(**inputs):
    import numpy as np
    import concourse.bacc as bacc
    from concourse.bass_utils import run_bass_kernel_spmd as run

    nc = bacc.Bacc("TRN2", target_bir_lowering=False, num_devices=1)
    arrays, io = {}, {}
    for name in _INS:
        a = np.ascontiguousarray(inputs[name])
        arrays["in_" + name] = a
        io[name] = nc.dram_tensor("in_" + name, a.shape, mybir.dt.from_np(a.dtype), kind="ExternalInput").ap()
    a = distance_buckets()
    arrays["in_bucket_of_distance"] = a
    io["bucket_of_distance"] = nc.dram_tensor("in_bucket_of_distance", a.shape, F32, kind="ExternalInput").ap()
    out = nc.dram_tensor("out", (1, SEQ, D), F32, kind="ExternalOutput").ap()
    build(nc, io, out)
    return run(nc, [arrays], core_ids=[0]).results[0]["out"]
```
